# Optimizing a Trainium2 kernel written in Bass

```python
import math
import jax
import jax.numpy as jnp
from jax import lax
import numpy as np

D_MODEL = 1024
BATCH = 1
SEQ = 512
DEPTH = 2

GRID_W = 64
CTX_LEN = 256
EPS = 1e-6
LRU_WIDTH = D_MODEL // 2
LRU_BLOCKS = 8
LRU_BLOCK_W = LRU_WIDTH // LRU_BLOCKS
LRU_C = 8.0
CONV_W = 4
CONV_LEFT = 2
ATT_HEADS = 4
ATT_DH = 64
ATT_DV = 2 * ATT_DH
ATT_QK_W = ATT_HEADS * 2 * ATT_DH
ATT_WIDTH = ATT_HEADS * ATT_DV
Q_BLOCK = 128
ROPE_BASE = 10000.0
EVEN_IN = 2 * LRU_WIDTH + 2 * ATT_QK_W + ATT_WIDTH
EVEN_MIX = LRU_WIDTH + ATT_WIDTH
S5_GROUP = 16
S5_GROUPS = D_MODEL // S5_GROUP
S5_STATE = 64
S5_CHUNK = 128
N_EXPERTS = 64
TOP_K = 6
D_EXPERT = 256
ROUTED_SCALE = 2.5
MOE_BLOCK = 128

kernel_name = 'hybrid_rglru_diffattn_s5_moe_prefix_dit'

def rms_norm(x, g):
    xf = x.astype(jnp.float32)
    y = xf * lax.rsqrt(jnp.mean(xf * xf, axis=-1, keepdims=True) + EPS)
    return (y * g.astype(jnp.float32)).astype(x.dtype)

def modulate(x, shift, scale):
    return x * (1 + scale) + shift

def swiglu(x, w_gate, w_up, w_down):
    return (jax.nn.silu(x @ w_gate) * (x @ w_up)) @ w_down

def linear_scan(a, b, h0, reverse):
    first = -1 if reverse else 0
    b = b.at[:, first].add(a[:, first] * h0)

    def combine(left, right):
        a_l, b_l = left
        a_r, b_r = right
        return a_l * a_r, a_r * b_l + b_r

    _, h = lax.associative_scan(combine, (a, b), axis=1, reverse=reverse)
    return h, (h[:, 0] if reverse else h[:, -1])

def centred_depthwise_conv(x, w, b):
    n = x.shape[1]
    xp = jnp.pad(x, ((0, 0), (CONV_LEFT, CONV_W - 1 - CONV_LEFT), (0, 0)))
    out = xp[:, 0:n] * w[0]
    for k in range(1, CONV_W):
        out = out + xp[:, k:k + n] * w[k]
    return out + b

def rglru_coeffs(x, lam, r_w, r_b, i_w, i_b):
    xf = x.astype(jnp.float32)
    xb = xf.reshape(xf.shape[:-1] + (LRU_BLOCKS, LRU_BLOCK_W))

    def block_diag(w, bias):
        y = jnp.einsum('blnd,nde->blne', xb, w.astype(jnp.float32))
        return y.reshape(xf.shape) + bias.astype(jnp.float32)

    r = jax.nn.sigmoid(block_diag(r_w, r_b))
    i = jax.nn.sigmoid(block_diag(i_w, i_b))
    log_a = -LRU_C * r * jax.nn.softplus(-lam.astype(jnp.float32))
    a = jnp.exp(log_a)
    b = jnp.sqrt(-jnp.expm1(2.0 * log_a)) * (i * xf)
    return a, b

def bi_rglru(x_lat, x_ctx, lam, r_w, r_b, i_w, i_b):
    y_lat = 0.0
    y_ctx = 0.0
    for d, rev in enumerate((False, True)):
        a_c, b_c = rglru_coeffs(x_ctx, lam[d], r_w[d], r_b[d], i_w[d], i_b[d])
        h0 = jnp.zeros((x_ctx.shape[0], LRU_WIDTH), jnp.float32)
        h_c, h_last = linear_scan(a_c, b_c, h0, rev)
        a_l, b_l = rglru_coeffs(x_lat, lam[d], r_w[d], r_b[d], i_w[d], i_b[d])
        h_l, _ = linear_scan(a_l, b_l, h_last, rev)
        y_lat = y_lat + h_l
        y_ctx = y_ctx + h_c
    return y_lat, y_ctx

def axial_rope_tables(rows):
    r, col = jnp.meshgrid(jnp.arange(rows), jnp.arange(GRID_W), indexing='ij')
    pos = jnp.stack([r.reshape(-1), col.reshape(-1)], axis=-1).astype(jnp.float32)
    n_freq = ATT_DH // 4
    inv_freq = ROPE_BASE ** (-jnp.arange(n_freq, dtype=jnp.float32) / n_freq)
    ang = pos[:, :, None] * inv_freq
    return jnp.cos(ang), jnp.sin(ang)

def apply_axial_rope(x, cos, sin):
    shp = x.shape
    xr = x.reshape(shp[:-1] + (2, 2, ATT_DH // 4))
    x1, x2 = xr[..., 0, :], xr[..., 1, :]
    c = cos[:, None, None].astype(x.dtype)
    s = sin[:, None, None].astype(x.dtype)
    return jnp.stack([x1 * c - x2 * s, x2 * c + x1 * s], axis=-2).reshape(shp)

def diff_attend(q, k, v, lam):
    s = jnp.einsum('bqhmd,bkhmd->bhmqk', q, k).astype(jnp.float32) * (ATT_DH ** -0.5)
    p = jax.nn.softmax(s, axis=-1)
    p = p[:, :, 0] - lam * p[:, :, 1]
    return jnp.einsum('bhqk,bkhd->bqhd', p.astype(v.dtype), v)

def rglru_diffattn_mixer(h, hc, w_in, w_out, conv_w, conv_b, lru_lam, lru_r_w, lru_r_b, lru_i_w, lru_i_b,
                         q_g, k_g, lam_q1, lam_k1, lam_q2, lam_k2, subln_g, lam_init, cos, sin, need_ctx):
    f32 = jnp.float32
    bsz, n, _ = h.shape
    n_c = hc.shape[1]
    cuts = [LRU_WIDTH, 2 * LRU_WIDTH, 2 * LRU_WIDTH + ATT_QK_W, 2 * LRU_WIDTH + 2 * ATT_QK_W]
    gate, xa, q, k, v = jnp.split(h @ w_in, cuts, axis=-1)
    gate_c, xa_c, q_c, k_c, v_c = jnp.split(hc @ w_in, cuts, axis=-1)
    xa = centred_depthwise_conv(xa, conv_w, conv_b)
    xa_c = centred_depthwise_conv(xa_c, conv_w, conv_b)
    r_lat, r_ctx = bi_rglru(xa, xa_c, lru_lam, lru_r_w, lru_r_b, lru_i_w, lru_i_b)
    ya = (r_lat * jax.nn.gelu(gate.astype(f32))).astype(h.dtype)
    split_heads = lambda t: t.reshape(t.shape[:2] + (ATT_HEADS, 2, ATT_DH))
    q = apply_axial_rope(rms_norm(split_heads(q), q_g), cos, sin)
    k = apply_axial_rope(rms_norm(split_heads(k), k_g), cos, sin)
    k_c = rms_norm(split_heads(k_c), k_g)
    v = v.reshape(bsz, n, ATT_HEADS, ATT_DV)
    v_c = v_c.reshape(bsz, n_c, ATT_HEADS, ATT_DV)
    lam = (jnp.exp(jnp.sum(lam_q1.astype(f32) * lam_k1.astype(f32)))
           - jnp.exp(jnp.sum(lam_q2.astype(f32) * lam_k2.astype(f32))) + lam_init)
    k_all = jnp.concatenate([k_c, k], axis=1)
    v_all = jnp.concatenate([v_c, v], axis=1)
    n_blk = n // Q_BLOCK
    q_blocks = q.reshape(bsz, n_blk, Q_BLOCK, ATT_HEADS, 2, ATT_DH).swapaxes(0, 1)
    o = lax.map(lambda qb: diff_attend(qb, k_all, v_all, lam), q_blocks)
    o = o.swapaxes(0, 1).reshape(bsz, n, ATT_HEADS, ATT_DV)
    yb = (rms_norm(o, subln_g) * (1.0 - lam_init)).reshape(bsz, n, ATT_WIDTH)
    y = jnp.concatenate([ya, yb], axis=-1) @ w_out
    if not need_ctx:
        return y, None
    q_c = rms_norm(split_heads(q_c), q_g)
    o_c = diff_attend(q_c, k_c, v_c, lam)
    ya_c = (r_ctx * jax.nn.gelu(gate_c.astype(f32))).astype(h.dtype)
    yb_c = (rms_norm(o_c, subln_g) * (1.0 - lam_init)).reshape(bsz, n_c, ATT_WIDTH)
    y_c = jnp.concatenate([ya_c, yb_c], axis=-1) @ w_out
    return y, y_c

def s5_scan(u, lam_bar, b_bar, c_mat, h0, reverse, with_output):
    bsz, n, g, i = u.shape
    chunks = u.reshape(bsz, n // S5_CHUNK, S5_CHUNK, g, i).swapaxes(0, 1)

    def step(h, u_blk):
        bu = jnp.einsum('blgi,gpi->blgp', u_blk.astype(jnp.complex64), b_bar)
        a = jnp.broadcast_to(lam_bar, bu.shape)
        hs, h_last = linear_scan(a, bu, h, reverse)
        y = jnp.real(jnp.einsum('blgp,gip->blgi', hs, c_mat)) if with_output else None
        return h_last, y

    h_last, ys = lax.scan(step, h0, chunks, reverse=reverse)
    if with_output:
        ys = ys.swapaxes(0, 1).reshape(bsz, n, g, i)
    return ys, h_last

def s5_mixer(h, hc, a_re, a_im, log_step, b_re, b_im, c_re, c_im, d_skip, glu_w, glu_b, need_ctx):
    f32 = jnp.float32
    bsz, n, dm = h.shape
    grp = lambda t: t.astype(f32).reshape(t.shape[:2] + (S5_GROUPS, S5_GROUP))
    u, u_c = grp(h), grp(hc)
    d = d_skip.astype(f32).reshape(S5_GROUPS, S5_GROUP)
    y = u * d
    y_c = u_c * d if need_ctx else None
    for di, rev in enumerate((False, True)):
        lam = lax.complex(jnp.minimum(a_re[di].astype(f32), -1e-4), a_im[di].astype(f32))
        lam_bar = jnp.exp(lam * jnp.exp(log_step[di].astype(f32)))
        b_bar = ((lam_bar - 1.0) / lam)[..., None] * lax.complex(b_re[di].astype(f32), b_im[di].astype(f32))
        c_mat = lax.complex(c_re[di].astype(f32), c_im[di].astype(f32))
        h0 = jnp.zeros((bsz, S5_GROUPS, S5_STATE), jnp.complex64)
        yc_d, h_ctx = s5_scan(u_c, lam_bar, b_bar, c_mat, h0, rev, need_ctx)
        yl_d, _ = s5_scan(u, lam_bar, b_bar, c_mat, h_ctx, rev, True)
        y = y + yl_d
        if need_ctx:
            y_c = y_c + yc_d

    def glu(t):
        z = jax.nn.gelu(t.reshape(t.shape[:2] + (dm,))).astype(h.dtype)
        val, gt = jnp.split(z @ glu_w + glu_b, 2, axis=-1)
        return val * jax.nn.sigmoid(gt)

    return glu(y), (glu(y_c) if need_ctx else None)

def moe_ffn(h, router_w, router_bias, w_gate, w_up, w_down, ws_gate, ws_up, ws_down):
    n_tok, dm = h.shape
    f32 = jnp.float32
    affinity = jax.nn.sigmoid((h @ router_w).astype(f32))
    _, idx = lax.top_k(affinity + router_bias.astype(f32), TOP_K)
    s_sel = jnp.take_along_axis(affinity, idx, axis=-1)
    gates = s_sel / jnp.sum(s_sel, axis=-1, keepdims=True) * ROUTED_SCALE
    n_assign = n_tok * TOP_K
    e_flat = idx.reshape(-1)
    t_flat = jnp.repeat(jnp.arange(n_tok, dtype=jnp.int32), TOP_K)
    g_flat = gates.reshape(-1).astype(h.dtype)
    order = jnp.argsort(e_flat)
    e_s, t_s, g_s = e_flat[order], t_flat[order], g_flat[order]
    counts = jnp.bincount(e_flat, length=N_EXPERTS)
    padded = (counts + MOE_BLOCK - 1) // MOE_BLOCK * MOE_BLOCK
    pad_end = jnp.cumsum(padded)
    pad_start = pad_end - padded
    sort_start = jnp.cumsum(counts) - counts
    dest = pad_start[e_s] + jnp.arange(n_assign, dtype=jnp.int32) - sort_start[e_s]
    n_blocks = -(-(n_assign + N_EXPERTS * (MOE_BLOCK - 1)) // MOE_BLOCK)
    tok_pad = jnp.full((n_blocks * MOE_BLOCK,), n_tok, jnp.int32).at[dest].set(t_s)
    g_pad = jnp.zeros((n_blocks * MOE_BLOCK,), h.dtype).at[dest].set(g_s)
    blk_start = jnp.arange(n_blocks, dtype=jnp.int32) * MOE_BLOCK
    blk_expert = jnp.minimum(jnp.searchsorted(pad_end, blk_start, side='right'), N_EXPERTS - 1)
    h_ext = jnp.concatenate([h, jnp.zeros((1, dm), h.dtype)], axis=0)

    def expert_block(acc, blk):
        tok, g, e = blk
        y = swiglu(h_ext[tok], w_gate[e], w_up[e], w_down[e])
        return acc.at[tok].add(y * g[:, None]), None

    acc, _ = lax.scan(expert_block, jnp.zeros_like(h_ext),
                      (tok_pad.reshape(n_blocks, MOE_BLOCK), g_pad.reshape(n_blocks, MOE_BLOCK), blk_expert))
    return acc[:n_tok] + swiglu(h, ws_gate, ws_up, ws_down)

def setup_inputs(seed: int = 0) -> dict:
    key = jax.random.key(seed)
    keys = iter(jax.random.split(key, 64))
    f32 = jnp.float32
    dm = D_MODEL
    n_even = (DEPTH + 1) // 2
    n_odd = DEPTH // 2

    def normal(shape, scale):
        return jax.random.normal(next(keys), shape, f32) * scale

    def gain(shape):
        return 1.0 + normal(shape, 0.02)

    def uniform(shape, lo, hi):
        return jax.random.uniform(next(keys), shape, f32, lo, hi)

    a8 = uniform((n_even, 2, LRU_WIDTH), 0.9, 0.999)
    a_lru = a8 ** (1.0 / LRU_C)
    s5_n = jnp.arange(S5_STATE, dtype=f32)
    s5_shape = (n_odd, 2, S5_GROUPS, S5_STATE)
    return {
        'x': normal((BATCH, SEQ, dm), 1.0),
        'c': normal((BATCH, dm), 1.0),
        'ctx': normal((BATCH, CTX_LEN, dm), 1.0),
        'c_ctx': normal((dm,), 1.0),
        'mod_w': normal((DEPTH, dm, 6 * dm), 0.5 * dm ** -0.5),
        'mod_b': normal((DEPTH, 6 * dm), 0.02),
        'norm1_g': gain((DEPTH, dm)),
        'norm2_g': gain((DEPTH, dm)),
        'ar_w_in': normal((n_even, dm, EVEN_IN), dm ** -0.5),
        'ar_w_out': normal((n_even, EVEN_MIX, dm), EVEN_MIX ** -0.5),
        'lru_conv_w': normal((n_even, CONV_W, LRU_WIDTH), CONV_W ** -0.5),
        'lru_conv_b': normal((n_even, LRU_WIDTH), 0.02),
        'lru_lam': jnp.log(a_lru) - jnp.log1p(-a_lru),
        'lru_r_w': normal((n_even, 2, LRU_BLOCKS, LRU_BLOCK_W, LRU_BLOCK_W), LRU_BLOCK_W ** -0.5),
        'lru_r_b': normal((n_even, 2, LRU_WIDTH), 0.02),
        'lru_i_w': normal((n_even, 2, LRU_BLOCKS, LRU_BLOCK_W, LRU_BLOCK_W), LRU_BLOCK_W ** -0.5),
        'lru_i_b': normal((n_even, 2, LRU_WIDTH), 0.02),
        'attn_q_g': gain((n_even, ATT_DH)),
        'attn_k_g': gain((n_even, ATT_DH)),
        'attn_lam_q1': normal((n_even, ATT_DH), 0.1),
        'attn_lam_k1': normal((n_even, ATT_DH), 0.1),
        'attn_lam_q2': normal((n_even, ATT_DH), 0.1),
        'attn_lam_k2': normal((n_even, ATT_DH), 0.1),
        'attn_subln_g': gain((n_even, ATT_DV)),
        's5_a_re': -0.5 + normal(s5_shape, 0.01),
        's5_a_im': math.pi * s5_n + normal(s5_shape, 0.01),
        's5_log_step': uniform(s5_shape, math.log(1e-3), math.log(1e-1)),
        's5_b_re': normal(s5_shape + (S5_GROUP,), (2 * S5_GROUP) ** -0.5),
        's5_b_im': normal(s5_shape + (S5_GROUP,), (2 * S5_GROUP) ** -0.5),
        's5_c_re': normal((n_odd, 2, S5_GROUPS, S5_GROUP, S5_STATE), (2 * S5_STATE) ** -0.5),
        's5_c_im': normal((n_odd, 2, S5_GROUPS, S5_GROUP, S5_STATE), (2 * S5_STATE) ** -0.5),
        's5_d': normal((n_odd, dm), 1.0),
        's5_glu_w': normal((n_odd, dm, 2 * dm), dm ** -0.5),
        's5_glu_b': normal((n_odd, 2 * dm), 0.02),
        'router_w': normal((DEPTH, dm, N_EXPERTS), dm ** -0.5),
        'router_bias': normal((DEPTH, N_EXPERTS), 0.01),
        'exp_w_gate': normal((DEPTH, N_EXPERTS, dm, D_EXPERT), dm ** -0.5),
        'exp_w_up': normal((DEPTH, N_EXPERTS, dm, D_EXPERT), dm ** -0.5),
        'exp_w_down': normal((DEPTH, N_EXPERTS, D_EXPERT, dm), D_EXPERT ** -0.5),
        'sh_w_gate': normal((DEPTH, dm, D_EXPERT), dm ** -0.5),
        'sh_w_up': normal((DEPTH, dm, D_EXPERT), dm ** -0.5),
        'sh_w_down': normal((DEPTH, D_EXPERT, dm), D_EXPERT ** -0.5),
    }

def reference(x, c, ctx, c_ctx, mod_w, mod_b, norm1_g, norm2_g,
              ar_w_in, ar_w_out, lru_conv_w, lru_conv_b, lru_lam, lru_r_w, lru_r_b, lru_i_w, lru_i_b,
              attn_q_g, attn_k_g, attn_lam_q1, attn_lam_k1, attn_lam_q2, attn_lam_k2, attn_subln_g,
              s5_a_re, s5_a_im, s5_log_step, s5_b_re, s5_b_im, s5_c_re, s5_c_im, s5_d, s5_glu_w, s5_glu_b,
              router_w, router_bias, exp_w_gate, exp_w_up, exp_w_down, sh_w_gate, sh_w_up, sh_w_down):
    bsz, n, dm = x.shape
    rows = n // GRID_W
    cos, sin = axial_rope_tables(rows)
    mod_in = jax.nn.silu(c)
    mod_in_c = jax.nn.silu(c_ctx)
    for layer in range(DEPTH):
        last = layer == DEPTH - 1
        j = layer // 2
        m = (mod_in @ mod_w[layer] + mod_b[layer])[:, None, :]
        mc = mod_in_c @ mod_w[layer] + mod_b[layer]
        sh1, sc1, g1, sh2, sc2, g2 = jnp.split(m, 6, axis=-1)
        sh1c, sc1c, g1c, sh2c, sc2c, g2c = jnp.split(mc, 6, axis=-1)
        h = modulate(rms_norm(x, norm1_g[layer]), sh1, sc1)
        hc = modulate(rms_norm(ctx, norm1_g[layer]), sh1c, sc1c)
        if layer % 2 == 0:
            lam_init = 0.8 - 0.6 * math.exp(-0.3 * layer)
            y, y_c = rglru_diffattn_mixer(
                h, hc, ar_w_in[j], ar_w_out[j], lru_conv_w[j], lru_conv_b[j], lru_lam[j],
                lru_r_w[j], lru_r_b[j], lru_i_w[j], lru_i_b[j], attn_q_g[j], attn_k_g[j],
                attn_lam_q1[j], attn_lam_k1[j], attn_lam_q2[j], attn_lam_k2[j], attn_subln_g[j],
                lam_init, cos, sin, not last)
        else:
            y, y_c = s5_mixer(
                h, hc, s5_a_re[j], s5_a_im[j], s5_log_step[j], s5_b_re[j], s5_b_im[j],
                s5_c_re[j], s5_c_im[j], s5_d[j], s5_glu_w[j], s5_glu_b[j], not last)
        x = x + g1 * y
        moe_w = (router_w[layer], router_bias[layer], exp_w_gate[layer], exp_w_up[layer], exp_w_down[layer],
                 sh_w_gate[layer], sh_w_up[layer], sh_w_down[layer])
        h2 = modulate(rms_norm(x, norm2_g[layer]), sh2, sc2)
        if last:
            x = x + g2 * moe_ffn(h2.reshape(-1, dm), *moe_w).reshape(x.shape)
        else:
            ctx = ctx + g1c * y_c
            h2c = modulate(rms_norm(ctx, norm2_g[layer]), sh2c, sc2c)
            n_ctx_tok = h2c.shape[0] * h2c.shape[1]
            out = moe_ffn(jnp.concatenate([h2c.reshape(-1, dm), h2.reshape(-1, dm)], axis=0), *moe_w)
            ctx = ctx + g2c * out[:n_ctx_tok].reshape(ctx.shape)
            x = x + g2 * out[n_ctx_tok:].reshape(x.shape)
    return x


_drawn_inputs = setup_inputs


def setup_inputs(seed=0):
    import zlib

    import numpy as np

    out = dict(_drawn_inputs(seed))
    spreads = {}
    factors = {'lru_r_b': 5.077,
     'lru_i_b': 3.162,
     'attn_q_g': 4.468,
     'attn_k_g': 4.355,
     'attn_lam_q1': 4.168,
     'attn_lam_k1': 4.568,
     'attn_lam_k2': 4.562,
     's5_a_re': 8.0,
     's5_b_re': 3.075,
     's5_b_im': 2.679,
     's5_c_re': 3.106,
     's5_c_im': 2.671,
     's5_glu_b': 4.81}
    for name, (base, spread) in spreads.items():
        noise = np.random.default_rng([zlib.crc32(name.encode()), seed]).standard_normal(out[name].shape)
        drawn = base * np.exp(spread * noise) if base else spread * noise
        out[name] = jnp.asarray(drawn.astype(out[name].dtype))
    for name, factor in factors.items():
        out[name] = (out[name] * factor).astype(out[name].dtype)
    return out
```

```python
import math
from contextlib import ExitStack

import numpy as np

import concourse.bass as bass
from concourse import mybir

F32, BF16, I32, U32 = mybir.dt.float32, mybir.dt.bfloat16, mybir.dt.int32, mybir.dt.uint32
ALU = mybir.AluOpType
ACT = mybir.ActivationFunctionType
AX = mybir.AxisListType

P = 128
D = 1024
KD = D // P
FE = 256
EPS = 1e-6
TOP_K = 6
LRU_C = 8.0
LAM_INIT = 0.8 - 0.6 * math.exp(-0.3 * 0)
GRID_W = 64
ROPE_BASE = 10000.0
ROUTED_SCALE = 2.5
BIG = 4096


class Counter:

    def __init__(self, eng, sem):
        self.eng, self.sem, self.n = eng, sem, 0

    def __call__(self, instruction):
        instruction.then_inc(self.sem, 1)
        self.n += 1

    def wait(self):
        self.eng.wait_ge(self.sem, self.n)


def rope_tables():
    t = np.arange(512)
    pos = np.stack([t // GRID_W, t % GRID_W], axis=-1).astype(np.float32)
    n_freq = 16
    inv = np.float32(ROPE_BASE) ** (-np.arange(n_freq, dtype=np.float32) / np.float32(n_freq))
    ang = pos[:, :, None] * inv
    cos, sin = np.cos(ang), np.sin(ang)
    both = np.stack([np.stack([cos, cos], axis=2), np.stack([-sin, sin], axis=2)], axis=1)
    return np.ascontiguousarray(both.reshape(512, 2, 64).astype(np.float32))



LAT, CTX = 512, 256
NTOK = LAT + CTX
NL, NT0 = LAT // P, NTOK // P
LRU, LF = 512, 4
DH, DV, NH = 64, 128, 4
XLAT, XCTX = 0, LAT + 3
XPAD = LAT + CTX + 6


def mixer0(nc, io, st):
    x = st['x']
    ctx = ExitStack()
    with nc.cleanup_on_exit(), ctx:
        def sb(name, shape, dt=F32):
            return ctx.enter_context(nc.sbuf_tensor(f"{name}_a", shape, dt))

        def sem(name):
            return nc.alloc_semaphore(f"{name}_a")

        hT = sb("hT", [P, KD, NTOK])
        qT, kT = hT[:, 0:NH, :], hT[:, NH:2 * NH, :]
        W = sb("W", [P, 2, KD, 512])
        w_out = W[:].rearrange("p a k (two n) -> p (a k two n)", two=1).rearrange("p (k n) -> p k n", n=D)
        QK = sb("QK", [P, NT0, D])
        o = QK[:, 0:3, :].rearrange("p t d -> p (t d)").rearrange("p (t h d) -> p t h d", h=NH, d=DV)
        ybT = QK[:, 3:6, :].rearrange("p t d -> p (t d)").rearrange("p (h n) -> p h n", n=NTOK)
        V = sb("V", [P, NT0, NH * DV])
        xa = sb("xa", [P, 2, XPAD])
        xc = sb("xc", [P, LF, XPAD])
        gate = sb("gate", [P, LF, NTOK])
        hs = sb("hs", [P, LF, NTOK])
        RIAT = sb("RIAT", [P, 4, 2, NTOK])
        R, I, A, T = (RIAT[:, j] for j in range(4))
        flatR = RIAT[:].rearrange("p a b n -> p (a b) n")
        prob = [[flatR[:, 2 * b + m, :] for m in range(2)] for b in range(2)]
        probT = [flatR[:, 4 + b, :] for b in range(2)]
        sqt = RIAT[:, 3].rearrange("p b n -> p (b n)")
        ident = sb("ident", [P, P])
        g1 = xc[:].rearrange("p f n -> p (f n)")[:, 0:2 * D].rearrange("p (s d) -> p s d", s=2)
        modc = sb("modc", [P, 2, 2, KD])
        gcol = sb("gcol", [P, KD])
        ss = sb("ss", [P, NT0])
        pv = sb("pv", [11, LRU])
        pcol = sb("pcol", [P, LF, 11])
        decay = sb("decay", [P, LF, 2])
        sp1 = sb("sp1", [P, LF, 2])
        sp2 = sb("sp2", [P, LF, 2])
        bd = sb("bd", [P, 2, 2, LF, P])
        rope = sb("rope", [P, NL, 2, DH])
        gqk = sb("gqk", [P, 2, DH])
        ropeg = sb("ropeg", [P, 2, 2, NL, DH])
        lamv = sb("lamv", [P, 4, DH])
        lams = sb("lams", [P, 4])
        qss = sb("qss", [P, NT0, 16])
        nmax = sb("nmax", [P, 2, 2])
        nmx = sb("nmx", [P, 2, 2])
        den = sb("den", [P, 2, 2])
        rden = sb("rden", [P, 2, 2])
        subg = sb("subg", [P, DV])
        oss = sb("oss", [P, NT0, NH])
        ps = ctx.enter_context(nc.psum_tensor("ps_a", [P, 8 * 512], F32))

        def bank(b, n=512, at=0):
            return ps[:, b * 512 + at:b * 512 + at + n]

        x_in = [sem(f"x_in{t}") for t in range(NT0)]
        small_in, tables_in, rows_in, bd_zero, bd_in, g1_in, wout_in = (sem(n) for n in
                                                             ("small_in", "tables_in", "rows_in", "bd_zero", "bd_in", "g1_in", "wout_in"))
        w_in = [sem(f"w_in{b}") for b in range(2)]
        names = ("ident_done sq_done var_done sd_done hn_done hT_mm hT_act hT_dve pcol_mm pcol_done pads_done xa_mm "
                 "xa_done conv_done gate_mm gate_done lru_mm sig_done at_done b2_done sqrt_done tm_mm tm_done lru_done "
                 "qss_done qsd_done rope_done qkT_mm qkT_act qkT_dve s_mm max_done exp_done p_done pT_mm pT_done "
                 "o_mm o_done oss_done osd_done on_done oT_mm oT_done y_mm y_used decay_e decay_l decay_done "
                 "lam_sum lam_exp chain achain")
        S = {n: sem(n) for n in names.split()}
        block = ctx.enter_context(nc.Block())

        CHUNKS = [LRU, 0, 2 * LRU, 2 * LRU + 512, 2 * LRU + 1024]
        ROUNDS = [(0, 0), (0, 1), (1, 0), (1, 1)]
        UNITS = [(t, h) for t in range(NT0) for h in range(NH)]

        def key0(t):
            return 0 if t < NL else LAT

        @block.sync
        def _(sp):
            for t in range(NT0):
                src = io['x'][0, t * P:(t + 1) * P, :] if t < NL else io['ctx'][0, (t - NL) * P:(t - NL + 1) * P, :]
                sp.dma_start(x[:, t, :], src).then_inc(x_in[t], 16)
            for s in range(2):
                sp.dma_start(modc[:, s], io['modrow'][0, s, 0:2 * D].rearrange("(j p k) -> p j k", j=2, k=KD)).then_inc(small_in, 16)
            sp.dma_start(gcol[:], io['norm1_g'][0].rearrange("(p k) -> p k", k=KD)).then_inc(small_in, 16)
            sp.dma_start(pv[0:4, :], io['lru_conv_w'][0]).then_inc(rows_in, 16)
            sp.dma_start(pv[4:5, :], io['lru_conv_b']).then_inc(rows_in, 16)
            sp.dma_start(pv[5:7, :], io['lru_lam'][0]).then_inc(rows_in, 16)
            sp.dma_start(pv[7:9, :], io['lru_r_b'][0]).then_inc(rows_in, 16)
            sp.dma_start(pv[9:11, :], io['lru_i_b'][0]).then_inc(rows_in, 16)
            w = io['ar_w_in'][0].rearrange("(p k) n -> p k n", k=KD)
            for c, col in enumerate(CHUNKS):
                if c >= 2:
                    sp.wait_ge(*((S['xa_mm'], LF), (S['gate_mm'], LF), (S['tm_mm'], NT0))[c - 2])
                sp.dma_start(W[:, c % 2], w[:, :, col:col + 512]).then_inc(w_in[c % 2], 16)
                if c == 0:
                    sp.wait_ge(bd_zero, 1)
                    for ri, name in enumerate(('lru_r_w', 'lru_i_w')):
                        for half in range(2):
                            for d in range(2):
                                src = io[name][0, d].rearrange("(f two) a e -> two a f e", two=2)[half]
                                at = slice(64 * half, 64 * half + 64)
                                sp.dma_start(bd[at, ri, d, :, at], src).then_inc(bd_in, 16)
                    sp.dma_start(rope[:], io['rope'].rearrange("(t p) s e -> p t s e", p=P)).then_inc(tables_in, 16)
                    for j, n in enumerate(('attn_q_g', 'attn_k_g')):
                        sp.dma_start(gqk[:, j, :], io[n].to_broadcast([P, DH])).then_inc(tables_in, 16)
                    for j, n in enumerate(('attn_lam_q1', 'attn_lam_q2', 'attn_lam_k1', 'attn_lam_k2')):
                        sp.dma_start(lamv[:, j, :], io[n].to_broadcast([P, DH])).then_inc(tables_in, 16)
                    sp.dma_start(subg[:], io['attn_subln_g'].to_broadcast([P, DV])).then_inc(tables_in, 16)
            sp.wait_ge(S['lru_done'], 8)
            for s in range(2):
                sp.dma_start(g1[:, s, :], io['modrow'][0, s:s + 1, 2 * D:3 * D].to_broadcast([P, D])).then_inc(g1_in, 16)
            sp.wait_ge(S['tm_mm'], 3 * NT0)
            sp.dma_start(w_out, io['ar_w_out'][0].rearrange("(k p) n -> p k n", p=P)).then_inc(wout_in, 16)

        @block.gpsimd
        def _(pool):
            pool.memset(bd[:], 0.0).then_inc(bd_zero, 1)
            pool.memset(ident[:], 0.0).then_inc(S['pads_done'], 1)
            for b in range(2):
                for at, n in ((0, 2), (LAT + 2, 3), (XPAD - 1, 1)):
                    pool.memset(xa[:, b, at:at + n], 0.0).then_inc(S['pads_done'], 1)
            pool.wait_ge(S['pads_done'], 7)
            pool.affine_select(out=ident[:], in_=ident[:], compare_op=ALU.not_equal, fill=1.0, base=0,
                               pattern=[[-1, P]], channel_multiplier=1).then_inc(S['ident_done'], 1)

        @block.scalar
        def _(act):
            done = Counter(act, S['achain'])
            for t in range(NT0):
                act.wait_ge(x_in[t], 16)
                if t:
                    act.wait_ge(S['sq_done'], t)
                act.activation(hs[:, 0:2, :].rearrange("p a n -> p (a n)")[:, 0:D], x[:, t, :], ACT.Square,
                               accum_out=ss[:, t:t + 1]).then_inc(S['sq_done'], 1)
            act.wait_ge(S['var_done'], 1)
            act.activation(ss[:], ss[:], ACT.Sqrt).then_inc(S['sd_done'], 1)
            for k in range(1, KD, 2):
                act.wait_ge(S['hT_mm'], k + 1)
                pair = bank(2 * (k % 2), NTOK)
                for s, a, b in ((0, 0, LAT), (1, LAT, NTOK)):
                    act.activation(hT[:, k, a:b], pair[:, a:b], ACT.Identity, bias=modc[:, s, 0, k:k + 1],
                                   scale=modc[:, s, 1, k:k + 1]).then_inc(S['hT_act'], 1)
            act.wait_ge(S['decay_e'], 1)
            done(act.activation(sp2[:], sp2[:], ACT.Exp))
            done.wait()
            act.activation(sp2[:], sp2[:], ACT.Ln, bias=1.0).then_inc(S['decay_l'], 1)
            for f in range(LF):
                act.wait_ge(S['xa_mm'], f + 1)
                if f >= 2:
                    act.wait_ge(S['conv_done'], f - 1)
                else:
                    act.wait_ge(S['pads_done'], 7)
                pair = bank(4 + 2 * (f % 2), NTOK)
                act.activation(xa[:, f % 2, 2:2 + LAT], pair[:, 0:LAT], ACT.Copy).then_inc(S['xa_done'], 1)
                act.activation(xa[:, f % 2, LAT + 5:LAT + 5 + CTX], pair[:, LAT:NTOK], ACT.Copy).then_inc(S['xa_done'], 1)
            for f in range(LF):
                act.wait_ge(S['gate_mm'], f + 1)
                if f == 0:
                    act.wait_ge(S['hn_done'], NT0)
                act.activation(gate[:, f, :], bank(4 + 2 * (f % 2), NTOK), ACT.Gelu_apprx_tanh).then_inc(S['gate_done'], 1)

            def lru(r):
                d, fp = ROUNDS[r]
                for j in range(2):
                    for ri, dst in enumerate((R, I)):
                        n = r * 4 + j * 2 + ri
                        act.wait_ge(S['lru_mm'], n + 1)
                        if r:
                            act.wait_ge(S['lru_done'], 2 * r)
                        f = 2 * fp + j
                        act.activation(dst[:, j, :], bank(4 + 2 * (n % 2), NTOK), ACT.Sigmoid,
                                       bias=pcol[:, f, 7 + 2 * ri + d:8 + 2 * ri + d]).then_inc(S['sig_done'], 1)
                act.wait_ge(S['sig_done'], 4 * (r + 1))
                act.wait_ge(S['decay_done'], 1)
                for j in range(2):
                    f = 2 * fp + j
                    act.activation(A[:, j, :], R[:, j, :], ACT.Exp, scale=decay[:, f, d:d + 1]).then_inc(S['at_done'], 1)
                act.wait_ge(S['at_done'], 4 * r + 2)
                for j in range(2):
                    f = 2 * fp + j
                    act.activation(R[:, j, :], R[:, j, :], ACT.Tanh, scale=decay[:, f, d:d + 1]).then_inc(S['at_done'], 1)
                act.wait_ge(S['b2_done'], r + 1)
                act.activation(T[:, :, :], T[:, :, :], ACT.Sqrt, scale=-1.0).then_inc(S['sqrt_done'], 1)

            def token_tiles(c):
                for t in range(NT0):
                    n = c * NT0 + t
                    act.wait_ge(S['tm_mm'], n + 1)
                    dst = QK[:, t, c * 512:(c + 1) * 512] if c < 2 else V[:, t, :]
                    act.activation(dst, bank(n % 4), ACT.Copy).then_inc(S['tm_done'], 1)

            def qk_deviation(j):
                act.wait_ge(S['qss_done'], j + 1)
                act.activation(qss[:, :, 8 * j:8 * j + 8], qss[:, :, 8 * j:8 * j + 8], ACT.Sqrt).then_inc(S['qsd_done'], 1)

            lru(0)
            token_tiles(0)
            lru(1)
            token_tiles(1)
            qk_deviation(0)
            lru(2)
            token_tiles(2)
            qk_deviation(1)
            lru(3)
            for n in range(1, 8, 2):
                act.wait_ge(S['qkT_mm'], n + 1)
                act.activation(hT[:, n, :], bank(2 * (n % 4), NTOK), ACT.Copy).then_inc(S['qkT_act'], 1)
            act.wait_ge(S['lam_sum'], 1)
            act.activation(lams[:, 0:2], lams[:, 0:2], ACT.Exp).then_inc(S['lam_exp'], 1)

            def exps(u):
                t, _ = UNITS[u]
                k0 = key0(t)
                act.wait_ge(S['max_done'], u + 1)
                if u == 0:
                    act.wait_ge(S['lru_done'], 8)
                    act.wait_ge(S['rope_done'], 2)
                if u >= 2:
                    act.wait_ge(S['pT_mm'], u - 1)
                for m in range(2):
                    act.activation(prob[u % 2][m][:, k0:], bank(2 * m, NTOK)[:, k0:], ACT.Exp, bias=nmx[:, u % 2, m:m + 1],
                                   scale=DH ** -0.5, accum_out=den[:, u % 2, m:m + 1]).then_inc(S['exp_done'], 1)

            exps(0)
            for u, (t, _) in enumerate(UNITS):
                act.wait_ge(S['pT_mm'], u + 1)
                if u >= 2:
                    act.wait_ge(S['o_mm'], u - 1)
                act.activation(probT[u % 2][:, key0(t):], bank(4, NTOK)[:, key0(t):], ACT.Copy).then_inc(S['pT_done'], 1)
                if u + 1 < len(UNITS):
                    exps(u + 1)
            act.wait_ge(S['oss_done'], 1)
            act.activation(oss[:], oss[:], ACT.Sqrt).then_inc(S['osd_done'], 1)
            for t in range(NT0):
                act.wait_ge(S['oT_mm'], t + 1)
                act.activation(ybT[:, :, t * P:(t + 1) * P], bank(t % 2).rearrange("p (h n) -> p h n", n=P),
                               ACT.Copy).then_inc(S['oT_done'], 1)

        @block.vector
        def _(dve):
            done = Counter(dve, S['chain'])
            dve.wait_ge(small_in, 16 * 3)
            for s in range(2):
                done(dve.scalar_tensor_tensor(out=modc[:, s, 1, :], in0=modc[:, s, 1, :], scalar=1.0, in1=gcol[:],
                                              op0=ALU.add, op1=ALU.mult))
            dve.wait_ge(S['sq_done'], NT0)
            done(dve.tensor_scalar(ss[:], ss[:], 1.0 / D, EPS, ALU.mult, ALU.add))
            done.wait()
            dve.reciprocal(ss[:], ss[:]).then_inc(S['var_done'], 1)
            dve.wait_ge(S['sd_done'], 1)
            for t in range(NT0):
                dve.tensor_scalar(QK[:, t, :], x[:, t, :], ss[:, t:t + 1], None, ALU.mult).then_inc(S['hn_done'], 1)
            for k in range(0, KD, 2):
                dve.wait_ge(S['hT_mm'], k + 1)
                pair = bank(2 * (k % 2), NTOK)
                for s, a, b in ((0, 0, LAT), (1, LAT, NTOK)):
                    dve.tensor_scalar(hT[:, k, a:b], pair[:, a:b], modc[:, s, 1, k:k + 1], modc[:, s, 0, k:k + 1],
                                      ALU.mult, ALU.add).then_inc(S['hT_dve'], 1)
            dve.wait_ge(S['pcol_mm'], 1)
            dve.tensor_copy(pcol[:], bank(4, LF * 11).rearrange("p (f v) -> p f v", v=11)).then_inc(S['pcol_done'], 1)
            dve.wait_ge(S['pcol_done'], 1)
            done(dve.tensor_scalar(sp1[:], pcol[:, :, 5:7], -1.0, None, ALU.mult))
            done.wait()
            done(dve.tensor_tensor(sp2[:], sp1[:], pcol[:, :, 5:7], ALU.min))
            done(dve.tensor_scalar(sp1[:], sp1[:], 0.0, None, ALU.max))
            done.wait()
            dve.sem_inc(S['decay_e'], 1)
            dve.wait_ge(S['decay_l'], 1)
            done(dve.tensor_tensor(sp1[:], sp1[:], sp2[:], ALU.add))
            done.wait()
            dve.tensor_scalar(decay[:], sp1[:], -LRU_C, None, ALU.mult).then_inc(S['decay_done'], 1)
            for f in range(LF):
                dve.wait_ge(S['xa_done'], 2 * f + 2)
                src, dst = xa[:, f % 2, :], xc[:, f, 0:XPAD - 3]
                done(dve.tensor_scalar(dst, src[:, 0:XPAD - 3], pcol[:, f, 0:1], pcol[:, f, 4:5], ALU.mult, ALU.add))
                for k in range(1, 4):
                    done.wait()
                    ins = dve.scalar_tensor_tensor(out=dst, in0=src[:, k:k + XPAD - 3], scalar=pcol[:, f, k:k + 1], in1=dst,
                                                   op0=ALU.mult, op1=ALU.add)
                    if k < 3:
                        done(ins)
                ins.then_inc(S['conv_done'], 1)

            def lru(r):
                d, fp = ROUNDS[r]
                fs = slice(2 * fp, 2 * fp + 2)
                dve.wait_ge(S['conv_done'], LF)
                dve.wait_ge(S['sig_done'], 4 * (r + 1))
                done(dve.tensor_tensor(I[:, :, 0:LAT], I[:, :, 0:LAT], xc[:, fs, XLAT:XLAT + LAT], ALU.mult))
                done(dve.tensor_tensor(I[:, :, LAT:], I[:, :, LAT:], xc[:, fs, XCTX:XCTX + CTX], ALU.mult))
                dve.wait_ge(S['at_done'], 4 * (r + 1))
                done(dve.tensor_tensor(T[:, :, :], A[:, :, :], A[:, :, :], ALU.mult))
                done.wait()
                dve.scalar_tensor_tensor(out=T[:, :, :], in0=T[:, :, :], scalar=1.0, in1=R[:, :, :], op0=ALU.add,
                                         op1=ALU.mult).then_inc(S['b2_done'], 1)
                dve.wait_ge(S['sqrt_done'], r + 1)
                done(dve.tensor_tensor(I[:, :, :], I[:, :, :], T[:, :, :], ALU.mult))
                done.wait()
                dst = hs[:, fs, :] if d == 0 else T
                for a, b in ((LAT, NTOK), (0, LAT)):
                    for j in range(2):
                        if d == 0:
                            at, before = slice(a, b), NTOK - 1
                        else:
                            at, before = slice(b - 1, a - 1 if a else None, -1), LAT
                        done(dve.tensor_tensor_scan(dst[:, j, at], A[:, j, at], I[:, j, at],
                                                    0.0 if a else dst[:, j, before:before + 1], ALU.mult, ALU.add))
                    done.wait()
                if d == 0:
                    dve.sem_inc(S['lru_done'], 2)
                else:
                    done(dve.tensor_tensor(hs[:, fs, :], hs[:, fs, :], T[:, :, :], ALU.add))
                    done.wait()
                    dve.wait_ge(S['gate_done'], LF)
                    dve.tensor_tensor(gate[:, fs, :], gate[:, fs, :], hs[:, fs, :], ALU.mult).then_inc(S['lru_done'], 2)

            def norm_rope(c):
                for t in range(NT0):
                    dve.wait_ge(S['tm_done'], c * NT0 + t + 1)
                    src = QK[:, t, c * 512:(c + 1) * 512]
                    tmp = scratch[:, 0:512]
                    done(dve.tensor_tensor(tmp, src, src, ALU.mult))
                    done.wait()
                    done(dve.tensor_reduce(qss[:, t, 8 * c:8 * c + 8], tmp.rearrange("p (h e) -> p h e", e=DH), AX.X, ALU.add))
                    done.wait()
                done(dve.tensor_scalar(qss[:, :, 8 * c:8 * c + 8], qss[:, :, 8 * c:8 * c + 8], 1.0 / DH, EPS, ALU.mult, ALU.add))
                done.wait()
                dve.reciprocal(qss[:, :, 8 * c:8 * c + 8], qss[:, :, 8 * c:8 * c + 8]).then_inc(S['qss_done'], 1)

            def finish_rope(c):
                dve.wait_ge(S['qsd_done'], c + 1)
                for t in range(NT0):
                    src = QK[:, t, c * 512:(c + 1) * 512].rearrange("p (h e) -> p h e", e=DH)
                    done(dve.tensor_tensor(src, src, qss[:, t:t + 1, 8 * c:8 * c + 8].rearrange("p o h -> p h o")
                                           .to_broadcast([P, 8, DH]), ALU.mult))
                done.wait()
                for t in range(NT0):
                    src = QK[:, t, c * 512:(c + 1) * 512].rearrange("p (h e) -> p h e", e=DH)
                    if t >= NL:
                        done(dve.tensor_tensor(src, src, gqk[:, c:c + 1, :].to_broadcast([P, 8, DH]), ALU.mult))
                        continue
                    tmp = scratch[:, 0:512].rearrange("p (h a s f) -> p h a s f", h=8, a=2, s=2)
                    half = QK[:, t, c * 512:(c + 1) * 512].rearrange("p (h a s f) -> p h a s f", h=8, a=2, s=2)
                    sin = ropeg[:, c, 1, t:t + 1, :].rearrange("p o (a s f) -> p o a s f", a=2, s=2)
                    done.wait()
                    for s in range(2):
                        done(dve.tensor_tensor(tmp[:, :, :, s, :], half[:, :, :, 1 - s, :],
                                               sin[:, :, :, s, :].to_broadcast([P, 8, 2, DH // 4]), ALU.mult))
                    done.wait()
                    done(dve.tensor_tensor(src, src, ropeg[:, c, 0, t:t + 1, :].to_broadcast([P, 8, DH]), ALU.mult))
                    done.wait()
                    done(dve.tensor_tensor(src, src, scratch[:, 0:512].rearrange("p (h e) -> p h e", e=DH), ALU.add))
                done.wait()
                dve.sem_inc(S['rope_done'], 1)

            dve.wait_ge(tables_in, 16 * 8)
            for c in range(2):
                g = gqk[:, c:c + 1, :]
                done(dve.tensor_tensor(ropeg[:, c, 0], rope[:, :, 0, :], g.to_broadcast([P, NL, DH]), ALU.mult))
                for s in range(2):
                    gs = g.rearrange("p o (a s f) -> p o a s f", a=2, s=2)[:, :, :, 1 - s, :].to_broadcast([P, NL, 2, DH // 4])
                    done(dve.tensor_tensor(
                        ropeg[:, c, 1].rearrange("p t (a s f) -> p t a s f", a=2, s=2)[:, :, :, s, :],
                        rope[:, :, 1, :].rearrange("p t (a s f) -> p t a s f", a=2, s=2)[:, :, :, s, :], gs, ALU.mult))
            done(dve.tensor_tensor(lamv[:, 0:2, :], lamv[:, 0:2, :], lamv[:, 2:4, :], ALU.mult))
            done.wait()
            dve.tensor_reduce(lams[:, 0:2], lamv[:, 0:2, :], AX.X, ALU.add).then_inc(S['lam_sum'], 1)
            scratch = xa[:, 0, :]
            lru(0)
            norm_rope(0)
            lru(1)
            norm_rope(1)
            finish_rope(0)
            lru(2)
            finish_rope(1)
            lru(3)
            for n in range(0, 8, 2):
                dve.wait_ge(S['qkT_mm'], n + 1)
                dve.tensor_copy(hT[:, n, :], bank(2 * (n % 4), NTOK)).then_inc(S['qkT_dve'], 1)
            dve.wait_ge(S['lam_exp'], 1)
            done(dve.tensor_tensor(lams[:, 2:3], lams[:, 1:2], lams[:, 0:1], ALU.subtract))
            done.wait()
            done(dve.tensor_scalar_add(lams[:, 3:4], lams[:, 2:3], -LAM_INIT))
            done(dve.tensor_scalar(subg[:], subg[:], 1.0 - LAM_INIT, None, ALU.mult))
            done.wait()

            def maxes(u):
                k0 = key0(UNITS[u][0])
                dve.wait_ge(S['s_mm'], u + 1)
                done(dve.tensor_reduce(nmax[:, u % 2, :], bank(0, 2048).rearrange("p (m n) -> p m n", m=2)[:, :, k0:NTOK],
                                       AX.X, ALU.max))
                done.wait()
                dve.tensor_scalar(nmx[:, u % 2, :], nmax[:, u % 2, :], -DH ** -0.5, None, ALU.mult).then_inc(S['max_done'], 1)

            def out_tile(u):
                t, h = UNITS[u]
                dve.wait_ge(S['o_mm'], u + 1)
                dve.tensor_copy(o[:, t, h, :], bank(6 + u % 2, DV)).then_inc(S['o_done'], 1)

            maxes(0)
            for u, (t, h) in enumerate(UNITS):
                k0, b = key0(t), u % 2
                dve.wait_ge(S['exp_done'], 2 * u + 2)
                done(dve.reciprocal(rden[:, b, :], den[:, b, :]))
                done.wait()
                done(dve.tensor_scalar(prob[b][1][:, k0:], prob[b][1][:, k0:], rden[:, b, 1:2], lams[:, 3:4],
                                       ALU.mult, ALU.mult))
                done.wait()
                dve.scalar_tensor_tensor(out=prob[b][0][:, k0:], in0=prob[b][0][:, k0:], scalar=rden[:, b, 0:1],
                                         in1=prob[b][1][:, k0:], op0=ALU.mult, op1=ALU.add).then_inc(S['p_done'], 1)
                if u:
                    out_tile(u - 1)
                if u + 1 < len(UNITS):
                    maxes(u + 1)
            out_tile(len(UNITS) - 1)
            dve.wait_ge(S['o_done'], len(UNITS))
            sq = flatR[:, 0:4, :].rearrange("p a n -> p (a n)").rearrange("p (t h d) -> p t h d", h=NH, d=DV)
            done(dve.tensor_tensor(sq, o, o, ALU.mult))
            done.wait()
            done(dve.tensor_reduce(oss[:], sq, AX.X, ALU.add))
            done.wait()
            done(dve.tensor_scalar(oss[:], oss[:], 1.0 / DV, EPS, ALU.mult, ALU.add))
            done.wait()
            dve.reciprocal(oss[:], oss[:]).then_inc(S['oss_done'], 1)
            dve.wait_ge(S['osd_done'], 1)
            for t in range(NT0):
                done(dve.tensor_tensor(o[:, t], o[:, t], oss[:, t, :].rearrange("p (h e) -> p h e", e=1)
                                       .to_broadcast([P, NH, DV]), ALU.mult))
                done.wait()
                dve.tensor_tensor(o[:, t], o[:, t], subg[:].rearrange("p (e d) -> p e d", e=1).to_broadcast([P, NH, DV]),
                                  ALU.mult).then_inc(S['on_done'], 1)
            dve.wait_ge(g1_in, 32)
            for t in range(NT0):
                s = 1 if t >= NL else 0
                dve.wait_ge(S['y_mm'], t + 1)
                tmp = flatR[:, 4 + 2 * (t % 2):6 + 2 * (t % 2), :].rearrange("p a n -> p (a n)")[:, 0:D]
                dve.tensor_tensor(tmp, bank(2 + 2 * (t % 2), D), g1[:, s, :], ALU.mult).then_inc(S['y_used'], 1)
                dve.wait_ge(S['y_used'], t + 1)
                done(dve.tensor_tensor(x[:, t, :], x[:, t, :], tmp, ALU.add))
            done.wait()

        @block.tensor
        def _(pe):
            pe.wait_ge(S['ident_done'], 1)
            for k in range(KD):
                if k == 0:
                    pe.wait_ge(S['hn_done'], NT0)
                if k >= 2:
                    pe.wait_ge(S['hT_act' if k % 2 else 'hT_dve'], 2 * (k // 2))
                for t in range(NT0):
                    last = pe.transpose(bank(2 * (k % 2), P, t * P), QK[:, t, :].rearrange("p (c k) -> p k c", k=KD)[:, k, :],
                                        ident[:])
                last.then_inc(S['hT_mm'], 1)
            pe.wait_ge(rows_in, 16 * 5)
            for f in range(LF):
                last = pe.transpose(bank(4, 11, f * 11), pv[:, f * P:(f + 1) * P], ident[0:11, 0:11])
            last.then_inc(S['pcol_mm'], 1)
            pe.wait_ge(S['hT_act'], KD)
            pe.wait_ge(S['hT_dve'], KD)

            def feature_chunk(c, mm, before):
                pe.wait_ge(w_in[c % 2], 16 * (c // 2 + 1))
                for f in range(LF):
                    before(f)
                    for a, b in ((0, LAT), (LAT, NTOK)):
                        for k in range(KD):
                            last = pe.matmul(bank(4 + 2 * (f % 2), b - a, a), W[:, c % 2, k, f * P:(f + 1) * P], hT[:, k, a:b],
                                             start=(k == 0), stop=(k == KD - 1))
                    last.then_inc(mm, 1)

            def before_xa(f):
                if f == 0:
                    pe.wait_ge(S['pcol_done'], 1)
                if f >= 2:
                    pe.wait_ge(S['xa_done'], 2 * (f - 1))

            def before_gate(f):
                if f < 2:
                    pe.wait_ge(S['xa_done'], 2 * (f + 3))
                else:
                    pe.wait_ge(S['gate_done'], f - 1)

            def lru(r):
                d, fp = ROUNDS[r]
                if r == 0:
                    pe.wait_ge(bd_in, 16 * 8)
                    pe.wait_ge(S['conv_done'], LF)
                for j in range(2):
                    for ri in range(2):
                        n, f = r * 4 + j * 2 + ri, 2 * fp + j
                        if n < 2:
                            pe.wait_ge(S['gate_done'], n + 3)
                        else:
                            pe.wait_ge(S['sig_done'], n - 1)
                        for at, x0, size in ((0, XLAT, LAT), (LAT, XCTX, CTX)):
                            last = pe.matmul(bank(4 + 2 * (n % 2), size, at), bd[:, ri, d, f, :], xc[:, f, x0:x0 + size],
                                             start=True, stop=True)
                        last.then_inc(S['lru_mm'], 1)

            def token_chunk(c):
                pe.wait_ge(w_in[c % 2], 16 * (c // 2 + 1))
                for t in range(NT0):
                    n = (c - 2) * NT0 + t
                    if n >= 4:
                        pe.wait_ge(S['tm_done'], n - 3)
                    for k in range(KD):
                        last = pe.matmul(bank(n % 4), hT[:, k, t * P:(t + 1) * P], W[:, c % 2, k, :],
                                         start=(k == 0), stop=(k == KD - 1))
                    last.then_inc(S['tm_mm'], 1)

            feature_chunk(0, S['xa_mm'], before_xa)
            feature_chunk(1, S['gate_mm'], before_gate)
            for r in range(3):
                lru(r)
                token_chunk(2 + r)
            lru(3)
            for n in range(8):
                c, h = divmod(n, NH)
                if n == 0:
                    pe.wait_ge(S['tm_done'], 3 * NT0)
                    pe.wait_ge(S['sig_done'], 16)
                pe.wait_ge(S['rope_done'], c + 1)
                if n >= 4:
                    pe.wait_ge(S['qkT_act' if n % 2 else 'qkT_dve'], n // 2 - 1)
                for t in range(NT0):
                    last = pe.transpose(bank(2 * (n % 4), P, t * P), QK[:, t, c * 512 + h * P:c * 512 + (h + 1) * P], ident[:])
                last.then_inc(S['qkT_mm'], 1)
            pe.wait_ge(S['qkT_act'], 4)
            pe.wait_ge(S['qkT_dve'], 4)

            def scores(u):
                t, h = UNITS[u]
                if u:
                    pe.wait_ge(S['exp_done'], 2 * u)
                for m in range(2):
                    at = slice(64 * m, 64 * m + 64)
                    for a, b in (((0, LAT),) if t < NL else ()) + ((LAT, NTOK),):
                        last = pe.matmul(bank(2 * m, b - a, a), qT[at, h, t * P:(t + 1) * P], kT[at, h, a:b],
                                         start=True, stop=True)
                last.then_inc(S['s_mm'], 1)

            scores(0)
            for u, (t, h) in enumerate(UNITS):
                if u + 1 < len(UNITS):
                    scores(u + 1)
                pe.wait_ge(S['p_done'], u + 1)
                if u:
                    pe.wait_ge(S['pT_done'], u)
                keys = range(0 if t < NL else NL, NT0)
                for kt in keys:
                    last = pe.transpose(bank(4, P, kt * P), prob[u % 2][0][:, kt * P:(kt + 1) * P], ident[:])
                last.then_inc(S['pT_mm'], 1)
                pe.wait_ge(S['pT_done'], u + 1)
                if u >= 2:
                    pe.wait_ge(S['o_done'], u - 1)
                for kt in keys:
                    last = pe.matmul(bank(6 + u % 2, DV), probT[u % 2][:, kt * P:(kt + 1) * P], V[:, kt, h * DV:(h + 1) * DV],
                                     start=(kt == keys[0]), stop=(kt == NT0 - 1))
                last.then_inc(S['o_mm'], 1)
            for t in range(NT0):
                pe.wait_ge(S['on_done'], t + 1)
                if t >= 2:
                    pe.wait_ge(S['oT_done'], t - 1)
                for h in range(NH):
                    last = pe.transpose(bank(t % 2, P, h * P), o[:, t, h, :], ident[:])
                last.then_inc(S['oT_mm'], 1)
            pe.wait_ge(wout_in, 16)
            pe.wait_ge(S['lru_done'], 8)
            for t in range(NT0):
                pe.wait_ge(S['oT_done'], t + 1)
                if t >= 2:
                    pe.wait_ge(S['y_used'], t - 1)
                for n in range(2):
                    for k in range(8):
                        rows = gate[:, k, t * P:(t + 1) * P] if k < LF else ybT[:, k - LF, t * P:(t + 1) * P]
                        last = pe.matmul(bank(2 + 2 * (t % 2) + n), rows, w_out[:, k, n * 512:(n + 1) * 512],
                                         start=(k == 0), stop=(k == 7))
                last.then_inc(S['y_mm'], 1)



def moe_blocks(nc, io, st, layer, n_tok, ctx_tiles):
    NT = n_tok // P
    NE = io['exp_w_gate'].shape[1]
    MAXB = NT
    NI = min(NE + (n_tok * TOP_K) // (P + 1), n_tok * TOP_K // P + NE)
    NI += -NI % 4
    assert NI + 3 <= P
    x = st['x']
    h_dram, acc_dram, tab_dram = st['moe_h'], st['moe_acc'], st['item_table']

    ctx = ExitStack()
    with nc.cleanup_on_exit(), ctx:
        def sb(name, shape, dt=F32):
            return ctx.enter_context(nc.sbuf_tensor(f"{name}_l{layer}", shape, dt))

        def sem(name):
            return nc.alloc_semaphore(f"{name}_l{layer}")

        rank = sb("rank", [P, NT, NE])
        pick_rhs = sb("pick_rhs", [P, NT, NE, 5], BF16)
        iota_slot = sb("iota_slot", [P, MAXB * P])
        table = sb("table", [1, P * 4], I32)
        ident = sb("ident", [P, P])
        moe_route(nc, io, st, layer, n_tok, ctx_tiles, rank, pick_rhs, iota_slot, table, ident)
        moe_loop(nc, io, st, layer, n_tok, NI, rank, pick_rhs, iota_slot, table, ident)
        moe_combine(nc, io, st, layer, n_tok, ctx_tiles)


def moe_route(nc, io, st, layer, n_tok, ctx_tiles, rank, pick_rhs, iota_slot, table, ident):
    NT = n_tok // P
    NE = io['exp_w_gate'].shape[1]
    MAXB = NT
    x, h_dram, acc_dram, tab_dram = st['x'], st['moe_h'], st['moe_acc'], st['item_table']
    streams = 2 if ctx_tiles else 1
    ctx = ExitStack()
    with nc.cleanup_on_exit(), ctx:
        def sb(name, shape, dt=F32):
            return ctx.enter_context(nc.sbuf_tensor(f"{name}_r{layer}", shape, dt))

        def ps(name, shape):
            return ctx.enter_context(nc.psum_tensor(f"{name}_r{layer}", shape, F32))

        def sem(name):
            return nc.alloc_semaphore(f"{name}_r{layer}")

        gain = sb("gain", [P, D])
        scale = sb("scale", [P, streams, D])
        shift = sb("shift", [P, streams, D])
        h = sb("h", [P, NT, D])
        hT = sb("hT", [P, KD, n_tok])
        junk = sb("junk", [P, D])
        ss = sb("ss", [P, NT])
        rw = sb("rw", [P, KD, NE])
        rbias = sb("rbias", [P, NE])
        aff = sb("aff", [P, NT, NE])
        sel = sb("sel", [P, NT, NE])
        top = sb("top", [P, NT, 8])
        topi = sb("topi", [P, NT, 8], U32)
        topf = sb("topf", [P, NT, 8])
        iota_e = sb("iota_e", [P, NE])
        hot = sb("hot", [P, NT, NE, TOP_K])
        mask = sb("mask", [P, NT, NE])
        maskb = sb("maskb", [P, NT, NE], BF16)
        gate = sb("gate", [P, NT, NE])
        gsum = sb("gsum", [P, NT])
        upper = sb("upper", [P, P], BF16)
        ones = sb("ones", [P, P], BF16)
        cnt = sb("cnt", [P, NE])
        nblk = sb("nblk", [P, NE])
        cumb = sb("cumb", [P, NE])
        item = sb("item", [P, 1])
        le = sb("le", [P, NE])
        tabf = sb("tabf", [P, 4])
        tabi = sb("tabi", [P, 4], I32)
        pid = sb("pid", [P, 1])
        wsgu = sb("wsgu", [P, 2, KD, FE])
        wsd = sb("wsd", [P, 2, D])
        hid = sb("hid", [P, 2, FE])
        hsil = sb("hsil", [P, 2, FE])
        hidT = sb("hidT", [P, 2, P])
        ysh = sb("ysh", [P, 2, D])
        pT = ps("pT", [P, 2, D // 2])
        pL = ps("pL", [P, NT * NE + NE])
        pGU = [ps(f"pGU{b}", [P, 2, FE]) for b in range(2)]
        pHT = ps("pHT", [P, 2, P])
        pY = ps("pY", [P, D])

        modload = sem("modload")
        wload = sem("wload")
        consts = sem("consts")
        sq_done = sem("sq_done")
        var_done = sem("var_done")
        sqrt_done = sem("sqrt_done")
        h_done = sem("h_done")
        trans_done = sem("trans_done")
        hT_done = sem("hT_done")
        logit_done = sem("logit_done")
        aff_done = sem("aff_done")
        mask_done = sem("mask_done")
        rank_mm = sem("rank_mm")
        tab_done = sem("tab_done")
        tab_out = sem("tab_out")
        tab_in = sem("tab_in")
        h_out = sem("h_out")
        gu_done = sem("gu_done")
        silu_done = sem("silu_done")
        hid_done = sem("hid_done")
        hidT_mm = sem("hidT_mm")
        hidT_done = sem("hidT_done")
        y_mm = sem("y_mm")
        y_done = sem("y_done")
        y_out = [sem(f"y_out{b}") for b in range(2)]
        chain = sem("chain")
        pchain = sem("pchain")
        block = ctx.enter_context(nc.Block())

        @block.sync
        def _(sp):
            mr = io['modrow'][layer]
            sp.dma_start(gain[:], io['norm2_g'][layer:layer + 1, :].to_broadcast([P, D])).then_inc(modload, 16)
            for s in range(streams):
                sp.dma_start(scale[:, s, :], mr[s:s + 1, 4 * D:5 * D].to_broadcast([P, D])).then_inc(modload, 16)
                sp.dma_start(shift[:, s, :], mr[s:s + 1, 3 * D:4 * D].to_broadcast([P, D])).then_inc(modload, 16)
            sp.dma_start(rw[:], io['router_w'][layer].rearrange("(p k) n -> p k n", k=KD)).then_inc(wload, 16)
            sp.dma_start(rbias[:], io['router_bias'][layer:layer + 1, :].to_broadcast([P, NE])).then_inc(wload, 16)
            sp.dma_start(wsgu[:, 0], io['sh_w_gate'][layer].rearrange("(p k) n -> p k n", k=KD)).then_inc(wload, 16)
            sp.dma_start(wsgu[:, 1], io['sh_w_up'][layer].rearrange("(p k) n -> p k n", k=KD)).then_inc(wload, 16)
            sp.dma_start(wsd[:], io['sh_w_down'][layer].rearrange("(p k) n -> p k n", k=2)).then_inc(wload, 16)
            for t in range(NT):
                sp.wait_ge(h_done, t + 1)
                sp.dma_start(h_dram[t * P:(t + 1) * P, :], h[:, t, :]).then_inc(h_out, 16)
            sp.wait_ge(tab_done, 1)
            sp.dma_start(tab_dram, tabi[:]).then_inc(tab_out, 16)
            sp.wait_ge(tab_out, 16)
            sp.dma_start(table[:], tab_dram.rearrange("(o a) b -> o (a b)", o=1)).then_inc(tab_in, 16)
            for t in range(NT):
                sp.wait_ge(y_done, t + 1)
                sp.dma_start(acc_dram[t * P:(t + 1) * P, :], ysh[:, t % 2, :]).then_inc(y_out[t % 2], 16)
            sp.wait_ge(h_out, 16 * NT)
            sp.wait_ge(tab_in, 16)
            for b in range(2):
                sp.wait_ge(y_out[b], 16 * (NT // 2))

        @block.gpsimd
        def _(pool):
            done = Counter(pool, pchain)
            done(pool.memset(ident[:], 0.0))
            done(pool.memset(upper[:], 1.0))
            pool.memset(ones[:], 1.0).then_inc(consts, 1)
            pool.iota(iota_e[:], [[1, NE]], base=0, channel_multiplier=0,
                      allow_small_or_imprecise_dtypes=True).then_inc(consts, 1)
            pool.iota(iota_slot[:], [[1, MAXB * P]], base=0, channel_multiplier=0,
                      allow_small_or_imprecise_dtypes=True).then_inc(consts, 1)
            pool.iota(item[:], [[0, 1]], base=0, channel_multiplier=1,
                      allow_small_or_imprecise_dtypes=True).then_inc(consts, 1)
            pool.iota(pick_rhs[:, :, :, 0], [[0, NT], [0, NE]], base=0, channel_multiplier=1,
                      allow_small_or_imprecise_dtypes=True).then_inc(consts, 1)
            pool.iota(pick_rhs[:, :, :, 1], [[P, NT], [0, NE]], base=-BIG, channel_multiplier=0,
                      allow_small_or_imprecise_dtypes=True).then_inc(consts, 1)
            done.wait()
            pool.affine_select(out=ident[:], in_=ident[:], compare_op=ALU.not_equal, fill=1.0, base=0,
                               pattern=[[-1, P]], channel_multiplier=1).then_inc(consts, 1)
            pool.affine_select(out=upper[:], in_=upper[:], compare_op=ALU.is_gt, fill=0.0, base=0,
                               pattern=[[1, P]], channel_multiplier=-1).then_inc(consts, 1)

        @block.scalar
        def _(act):
            for t in range(NT):
                if t:
                    act.wait_ge(sq_done, t)
                act.activation(junk[:], x[:, t, :], ACT.Square, accum_out=ss[:, t:t + 1]).then_inc(sq_done, 1)
            act.wait_ge(var_done, 1)
            act.activation(ss[:], ss[:], ACT.Sqrt).then_inc(sqrt_done, 1)
            for t in range(NT):
                for half in range(2):
                    act.wait_ge(trans_done, 2 * t + half + 1)
                    act.activation(hT[:, 4 * half:4 * half + 4, t * P:(t + 1) * P],
                                   pT[:, half].rearrange("p (k c) -> p k c", c=P), ACT.Copy).then_inc(hT_done, 1)
            act.wait_ge(logit_done, NT)
            act.activation(aff[:], pL[:, 0:NT * NE].rearrange("p (t e) -> p t e", e=NE), ACT.Sigmoid).then_inc(aff_done, 1)

            def silu(t):
                act.wait_ge(gu_done, t + 1)
                if t >= 2:
                    act.wait_ge(hid_done, t - 1)
                act.activation(hsil[:, t % 2], pGU[t % 2][:, 0, :], ACT.Silu).then_inc(silu_done, 1)

            silu(0)
            for t in range(NT):
                if t + 1 < NT:
                    silu(t + 1)
                act.wait_ge(hidT_mm, t + 1)
                act.activation(hidT[:], pHT[:], ACT.Copy).then_inc(hidT_done, 1)
                act.wait_ge(y_mm, t + 1)
                if t >= 2:
                    act.wait_ge(y_out[t % 2], 16 * (t // 2))
                act.activation(ysh[:, t % 2, :], pY[:], ACT.Copy).then_inc(y_done, 1)

        @block.vector
        def _(dve):
            done = Counter(dve, chain)
            dve.wait_ge(modload, 16 * (1 + 2 * streams))
            for s in range(streams):
                done(dve.scalar_tensor_tensor(out=scale[:, s, :], in0=scale[:, s, :], scalar=1.0, in1=gain[:],
                                              op0=ALU.add, op1=ALU.mult))
            dve.wait_ge(sq_done, NT)
            done(dve.tensor_scalar(ss[:], ss[:], 1.0 / D, EPS, ALU.mult, ALU.add))
            done.wait()
            dve.reciprocal(ss[:], ss[:]).then_inc(var_done, 1)
            dve.wait_ge(sqrt_done, 1)
            for t in range(NT):
                s = 1 if t >= NT - ctx_tiles else 0
                done(dve.scalar_tensor_tensor(out=h[:, t, :], in0=x[:, t, :], scalar=ss[:, t:t + 1],
                                              in1=scale[:, s, :], op0=ALU.mult, op1=ALU.mult))
                done.wait()
                dve.tensor_tensor(h[:, t, :], h[:, t, :], shift[:, s, :], ALU.add).then_inc(h_done, 1)

            def shared_hidden(t):
                dve.wait_ge(silu_done, t + 1)
                if t >= 2:
                    dve.wait_ge(hidT_mm, t - 1)
                dve.tensor_tensor(hid[:, t % 2], hsil[:, t % 2], pGU[t % 2][:, 1, :], ALU.mult).then_inc(hid_done, 1)

            dve.wait_ge(consts, 8)
            dve.wait_ge(wload, 80)
            dve.wait_ge(aff_done, 1)
            done(dve.tensor_tensor(sel[:], aff[:], rbias[:].rearrange("p (o e) -> p o e", o=1).to_broadcast([P, NT, NE]),
                                   ALU.add))
            done.wait()
            for t in range(NT):
                done(dve.max(top[:, t, :], sel[:, t, :]))
            done.wait()
            for t in range(NT):
                done(dve.max_index(topi[:, t, :], top[:, t, :], sel[:, t, :]))
            done.wait()
            done(dve.tensor_copy(topf[:], topi[:]))
            done.wait()
            for t in range(NT):
                done(dve.tensor_tensor(
                    hot[:, t], iota_e[:].rearrange("p (e o) -> p e o", o=1).to_broadcast([P, NE, TOP_K]),
                    topf[:, t:t + 1, 0:TOP_K].to_broadcast([P, NE, TOP_K]), ALU.is_equal))
            done.wait()
            done(dve.tensor_reduce(mask[:], hot[:], AX.X, ALU.add))
            done.wait()
            dve.tensor_copy(maskb[:], mask[:]).then_inc(mask_done, 1)
            shared_hidden(0)
            done(dve.tensor_tensor(gate[:], aff[:], mask[:], ALU.mult))
            done.wait()
            done(dve.tensor_reduce(gsum[:], gate[:], AX.X, ALU.add))
            done.wait()
            done(dve.reciprocal(gsum[:], gsum[:]))
            done.wait()
            done(dve.scalar_tensor_tensor(out=gate[:], in0=gate[:], scalar=ROUTED_SCALE,
                                          in1=gsum[:].rearrange("p (t o) -> p t o", o=1).to_broadcast([P, NT, NE]),
                                          op0=ALU.mult, op1=ALU.mult))
            done.wait()
            for part in range(3):
                done(dve.tensor_copy(pick_rhs[:, :, :, 2 + part], gate[:]))
                done.wait()
                if part < 2:
                    done(dve.tensor_tensor(gate[:], gate[:], pick_rhs[:, :, :, 2 + part], ALU.subtract))
                    done.wait()
            shared_hidden(1)
            shared_hidden(2)
            dve.wait_ge(rank_mm, 1)
            done(dve.scalar_tensor_tensor(out=rank[:], in0=pL[:, 0:NT * NE].rearrange("p (t e) -> p t e", e=NE),
                                          scalar=1.0, in1=mask[:], op0=ALU.add, op1=ALU.mult))
            done(dve.tensor_copy(cnt[:], pL[:, NT * NE:NT * NE + NE]))
            done.wait()
            done(dve.tensor_scalar_add(rank[:], rank[:], -1.0))
            done(dve.tensor_scalar(nblk[:], cnt[:], 0.0, None, ALU.is_gt))
            for b in range(1, MAXB):
                done.wait()
                done(dve.scalar_tensor_tensor(out=nblk[:], in0=cnt[:], scalar=float(b * P), in1=nblk[:],
                                              op0=ALU.is_gt, op1=ALU.add))
            done.wait()
            done(dve.tensor_tensor_scan(cumb[:], nblk[:], nblk[:], 0.0, ALU.add, ALU.bypass))
            done.wait()
            done(dve.tensor_scalar(le[:], cumb[:], item[:, 0:1], None, ALU.is_le))
            done.wait()
            done(dve.tensor_reduce(tabf[:, 0:1], le[:], AX.X, ALU.add))
            done(dve.tensor_tensor(nblk[:], nblk[:], le[:], ALU.mult))
            done.wait()
            done(dve.tensor_scalar(tabf[:, 0:1], tabf[:, 0:1], float(NE - 1), None, ALU.min))
            done(dve.tensor_reduce(tabf[:, 1:2], nblk[:], AX.X, ALU.add))
            done(dve.tensor_copy(tabf[:, 2:3], cumb[:, NE - 1:NE]))
            done(dve.tensor_copy(tabf[:, 3:4], cumb[:, NE - 1:NE]))
            done.wait()
            done(dve.tensor_tensor(tabf[:, 1:2], item[:], tabf[:, 1:2], ALU.subtract))
            done.wait()
            done(dve.tensor_scalar(tabf[:, 1:2], tabf[:, 1:2], float(MAXB - 1), float(P), ALU.min, ALU.mult))
            done.wait()
            dve.tensor_copy(tabi[:], tabf[:]).then_inc(tab_done, 1)
            for t in range(3, NT):
                shared_hidden(t)

        @block.tensor
        def _(pe):
            pe.wait_ge(consts, 8)
            pe.wait_ge(wload, 80)
            for t in range(NT):
                pe.wait_ge(h_done, t + 1)
                hk = h[:, t, :].rearrange("p (c k) -> p k c", k=KD)
                for half in range(2):
                    if t:
                        pe.wait_ge(hT_done, 2 * t + half - 1)
                    for k in range(4):
                        last = pe.transpose(pT[:, half, k * P:(k + 1) * P], hk[:, 4 * half + k, :], ident[:])
                    last.then_inc(trans_done, 1)
            for t in range(NT):
                pe.wait_ge(hT_done, 2 * t + 2)
                for k in range(KD):
                    last = pe.matmul(pL[:, t * NE:(t + 1) * NE], hT[:, k, t * P:(t + 1) * P], rw[:, k, :],
                                     start=(k == 0), stop=(k == KD - 1))
                last.then_inc(logit_done, 1)

            def gate_up(t):
                if t >= 2:
                    pe.wait_ge(hid_done, t - 1)
                for k in range(KD):
                    last = pe.matmul(pGU[t % 2][:], hT[:, k, t * P:(t + 1) * P], wsgu[:, :, k, :],
                                     start=(k == 0), stop=(k == KD - 1))
                last.then_inc(gu_done, 1)

            def down(t):
                pe.wait_ge(hid_done, t + 1)
                if t:
                    pe.wait_ge(hidT_done, t)
                for k in range(2):
                    last = pe.transpose(pHT[:, k, :], hid[:, t % 2, :].rearrange("p (c k) -> p k c", k=2)[:, k, :],
                                        ident[:])
                last.then_inc(hidT_mm, 1)
                pe.wait_ge(hidT_done, t + 1)
                if t:
                    pe.wait_ge(y_done, t)
                for n in range(2):
                    for k in range(2):
                        last = pe.matmul(pY[:, n * 512:(n + 1) * 512], hidT[:, k, :], wsd[:, k, n * 512:(n + 1) * 512],
                                         start=(k == 0), stop=(k == 1))
                last.then_inc(y_mm, 1)

            def ranks():
                pe.wait_ge(mask_done, 1)
                pe.wait_ge(aff_done, 1)
                for t in range(NT + 1):
                    col = pL[:, t * NE:(t + 1) * NE]
                    for u in range(min(t + 1, NT)):
                        last = pe.matmul(col, (upper if u == t else ones)[:], maskb[:, u, :],
                                         start=(u == 0), stop=(u == min(t + 1, NT) - 1))
                last.then_inc(rank_mm, 1)

            gate_up(0)
            for t in range(NT):
                if t + 1 < NT:
                    gate_up(t + 1)
                down(t)
                if t == 1:
                    ranks()


def moe_loop(nc, io, st, layer, n_tok, NI, rank, pick_rhs, iota_slot, table, ident):
    NT = n_tok // P
    NE = io['exp_w_gate'].shape[1]
    h_dram, acc_dram = st['moe_h'], st['moe_acc']
    w_gate, w_up, w_down = (io[n][layer] for n in ('exp_w_gate', 'exp_w_up', 'exp_w_down'))
    ctx = ExitStack()
    with nc.cleanup_on_exit(), ctx:
        def sb(name, shape, dt=F32):
            return ctx.enter_context(nc.sbuf_tensor(f"{name}_m{layer}", shape, dt))

        def ps(name, shape):
            return ctx.enter_context(nc.psum_tensor(f"{name}_m{layer}", shape, F32))

        def sem(name):
            return nc.alloc_semaphore(f"{name}_m{layer}")

        wgu = [sb(f"wgu{b}", [P, 2, KD, FE]) for b in range(4)]
        wd = [sb(f"wd{b}", [P, 2, D]) for b in range(4)]
        onehot = sb("onehot", [P, NT, P], BF16)
        idx = [sb(f"idx{b}", [P, 1], I32) for b in range(4)]
        gslot = [sb(f"gslot{b}", [P, 1]) for b in range(4)]
        xg = [sb(f"xg{b}", [P, D]) for b in range(4)]
        xT = [sb(f"xT{b}", [P, KD, P]) for b in range(2)]
        hsil = sb("hsil", [P, FE])
        hid = sb("hid", [P, FE])
        hidT = sb("hidT", [P, 2, P])
        y = [sb(f"y{b}", [P, D]) for b in range(2)]
        pGU = [ps(f"pGU{b}", [P, 2, FE]) for b in range(2)]
        pT = ps("pT", [P, D])
        pHT = ps("pHT", [P, 2, P])
        pI = ps("pI", [P, 8])
        pY = ps("pY", [P, D])

        gu_loaded = [sem(f"gu_loaded{b}") for b in range(4)]
        d_loaded = [sem(f"d_loaded{b}") for b in range(4)]
        onehot_done = sem("onehot_done")
        idx_mm = sem("idx_mm")
        idx_done = sem("idx_done")
        xg_zero = sem("xg_zero")
        gathered = [sem(f"gathered{b}") for b in range(4)]
        xT_mm = sem("xT_mm")
        xT_done = sem("xT_done")
        gu_mm = sem("gu_mm")
        silu_done = sem("silu_done")
        hid_done = sem("hid_done")
        hidT_mm = sem("hidT_mm")
        hidT_done = sem("hidT_done")
        y_mm = sem("y_mm")
        y_done = sem("y_done")
        y_added = [sem(f"y_added{b}") for b in range(2)]
        gate_sum = sem("gate_sum")
        pool_go = sem("pool_go")
        added = sem("added")
        id_sum = sem("id_sum")
        idf = sb("idf", [P, 1])
        block = ctx.enter_context(nc.Block())

        def n_items(eng):
            return eng.value_load(table[0:1, 2:3], min_val=1, max_val=NI)

        def items(eng, n, body):
            with eng.Fori(0, NI // 4) as q:
                for b in range(4):
                    with eng.If(n > q * 4 + b):
                        body(q * 4 + b, q, b)

        @block.sync
        def _(sp):
            def load(i, q, b):
                e = sp.value_load(table[0:1, bass.ds(i * 4, 1)], min_val=0, max_val=NE - 1)
                sp.wait_ge(gu_mm, i + 1)
                for j, w in enumerate((w_gate, w_up)):
                    sp.dma_start(wgu[b][:, j], w[bass.ds(e, 1)].rearrange("e (p k) n -> p (e k) n", k=KD))\
                      .then_inc(gu_loaded[b], 16)
                sp.wait_ge(y_mm, i + 1)
                sp.dma_start(wd[b][:], w_down[bass.ds(e, 1)].rearrange("e (p k) n -> p (e k) n", k=2))\
                  .then_inc(d_loaded[b], 16)
            items(sp, n_items(sp), load)

        @block.gpsimd
        def _(pool):
            last_row = pool.to_reg(n_tok - 1)

            def gather(b):
                pool.sem_inc(pool_go, 1)
                pool.indirect_dma_start(xg[b][:], None, h_dram,
                                        bass.IndirectOffsetOnAxis(idx[b][:].bitcast(U32), 0),
                                        bounds_check=last_row, oob_is_err=False).then_inc(gathered[b], 16)

            def item(i, q, b):
                if b:
                    pool.wait_ge(y_added[(b + 1) % 2], q * 32 + 16 * ((b + 1) // 2))
                else:
                    with pool.If(q > 0):
                        pool.wait_ge(y_added[1], q * 32)
                pool.sem_inc(added, 1)
                pool.wait_ge(idx_done, i + 5)
                pool.wait_ge(xT_mm, i + 1)
                gather((b + 3) % 4)
                pool.wait_ge(y_done, i + 2)
                pool.sem_inc(pool_go, 1)
                pool.indirect_dma_start(acc_dram, bass.IndirectOffsetOnAxis(idx[b][:].bitcast(U32), 0),
                                        y[b % 2][:], None, bounds_check=last_row, oob_is_err=False,
                                        compute_op=ALU.add).then_inc(y_added[b % 2], 16)

            for b in range(4):
                pool.memset(xg[b][:], 0.0).then_inc(xg_zero, 1)
            pool.wait_ge(xg_zero, 4)
            for b in range(3):
                pool.wait_ge(idx_done, b + 2)
                gather(b)
            n = n_items(pool)
            items(pool, n, item)
            pool.wait_ge(y_added[0], (n + 1) // 2 * 16)
            pool.wait_ge(y_added[1], n // 2 * 16)
            for b in range(4):
                pool.wait_ge(gathered[b], (n + 6 - b) // 4 * 16)

        @block.scalar
        def _(act):
            def evac_xT(b):
                act.activation(xT[b][:], pT[:].rearrange("p (k c) -> p k c", c=P), ACT.Copy).then_inc(xT_done, 1)

            def item(i, q, b):
                act.wait_ge(gu_mm, i + 5)
                act.wait_ge(hid_done, i + 1)
                act.activation(hsil[:], pGU[b % 2][:, 0, :], ACT.Silu).then_inc(silu_done, 1)
                act.wait_ge(xT_mm, i + 4)
                evac_xT(b % 2)
                act.wait_ge(y_mm, i + 5)
                act.wait_ge(added, i + 1)
                act.activation(y[b % 2][:], pY[:], ACT.Copy, scale=gslot[b][:]).then_inc(y_done, 1)

            act.sem_inc(y_done, 1)
            act.sem_inc(added, 1)
            for b in range(2):
                act.wait_ge(xT_mm, b + 2)
                evac_xT(b)
            items(act, n_items(act), item)

        @block.vector
        def _(dve):
            def mark(i):
                e = dve.value_load(table[0:1, bass.ds(i * 4, 1)], min_val=0, max_val=NE - 1)
                s0 = dve.value_load(table[0:1, bass.ds(i * 4 + 1, 1)], min_val=0, max_val=(NT - 1) * P)
                slots = iota_slot[:, bass.ds(s0, P)].rearrange("p (o s) -> p o s", o=1).to_broadcast([P, NT, P])
                dve.tensor_tensor(onehot[:], slots, rank[:, :, bass.ds(e, 1)].to_broadcast([P, NT, P]),
                                  ALU.is_equal).then_inc(onehot_done, 1)

            def tokens(i, b):
                dve.wait_ge(idx_mm, i + 1)
                dve.tensor_reduce(gslot[b][:], pI[:, 2:5], AX.X, ALU.add).then_inc(gate_sum, 1)
                dve.tensor_reduce(idf[:], pI[:, 0:2], AX.X, ALU.add).then_inc(id_sum, 1)
                dve.wait_ge(gate_sum, i + 1)
                dve.wait_ge(id_sum, i + 1)
                dve.tensor_scalar_add(idx[b][:], idf[:], float(BIG)).then_inc(idx_done, 1)

            def item(i, q, b):
                mark(i + 3)
                dve.wait_ge(silu_done, i + 1)
                dve.tensor_tensor(hid[:], hsil[:], pGU[b % 2][:, 1, :], ALU.mult).then_inc(hid_done, 1)
                dve.wait_ge(hidT_mm, i + 1)
                dve.wait_ge(y_mm, i + 4)
                dve.tensor_copy(hidT[:], pHT[:]).then_inc(hidT_done, 1)
                dve.wait_ge(added, i + 2)
                tokens(i + 3, (b + 3) % 4)

            for primed in (idx_done, hid_done, hidT_done):
                dve.sem_inc(primed, 1)
            for i in range(3):
                mark(i)
                tokens(i, i)
            items(dve, n_items(dve), item)

        @block.tensor
        def _(pe):
            def pick(i):
                e = pe.value_load(table[0:1, bass.ds(i * 4, 1)], min_val=0, max_val=NE - 1)
                pe.wait_ge(onehot_done, i + 1)
                pe.wait_ge(idx_done, i + 1)
                for t in range(NT):
                    last = pe.matmul(pI[:, 0:5], onehot[:, t, :], pick_rhs[:, t, bass.ds(e, 1), :]
                                     .rearrange("p e c -> p (e c)"), start=(t == 0), stop=(t == NT - 1))
                last.then_inc(idx_mm, 1)

            def transpose_rows(b):
                rows = xg[b][:].rearrange("p (c k) -> p k c", k=KD)
                for k in range(KD):
                    last = pe.transpose(pT[:, k * P:(k + 1) * P], rows[:, k, :], ident[:])
                last.then_inc(xT_mm, 1)

            def gate_up(b, xT_count, loaded, hid_count):
                pe.wait_ge(xT_done, xT_count)
                pe.wait_ge(gu_loaded[b], loaded)
                pe.wait_ge(hid_done, hid_count)
                for k in range(KD):
                    last = pe.matmul(pGU[b % 2][:], xT[b % 2][:, k, :], wgu[b][:, :, k, :],
                                     start=(k == 0), stop=(k == KD - 1))
                last.then_inc(gu_mm, 1)

            def item(i, q, b):
                with pe.If(n > q * 4 + (b + 1)):
                    gate_up((b + 1) % 4, i + 2, q * 32 + 32 * ((b + 1) // 4 + 1), i + 1)
                pe.wait_ge(hid_done, i + 2)
                pe.wait_ge(hidT_done, i + 1)
                for k in range(2):
                    last = pe.transpose(pHT[:, k, :], hid[:].rearrange("p (c k) -> p k c", k=2)[:, k, :], ident[:])
                last.then_inc(hidT_mm, 1)
                pe.wait_ge(gathered[(b + 2) % 4], q * 16 + 16 * ((b + 2) // 4 + 1))
                pe.wait_ge(xT_done, i + 2)
                transpose_rows((b + 2) % 4)
                pick(i + 3)
                pe.wait_ge(hidT_done, i + 2)
                pe.wait_ge(d_loaded[b], q * 16 + 16)
                pe.wait_ge(y_done, i + 1)
                for half in range(2):
                    for k in range(2):
                        last = pe.matmul(pY[:, half * 512:(half + 1) * 512], hidT[:, k, :],
                                         wd[b][:, k, half * 512:(half + 1) * 512], start=(k == 0), stop=(k == 1))
                last.then_inc(y_mm, 1)

            n = n_items(pe)
            pe.sem_inc(gu_mm, 4)
            pe.sem_inc(y_mm, 4)
            pe.sem_inc(xT_mm, 1)
            for i in range(3):
                pick(i)
            for b in range(2):
                pe.wait_ge(gathered[b], 16)
                if b:
                    pe.wait_ge(xT_done, b)
                transpose_rows(b)
            gate_up(0, 1, 32, 1)
            items(pe, n, item)


def moe_combine(nc, io, st, layer, n_tok, ctx_tiles):
    NT = n_tok // P
    x, acc_dram = st['x'], st['moe_acc']
    streams = 2 if ctx_tiles else 1
    ctx = ExitStack()
    with nc.cleanup_on_exit(), ctx:
        def sem(name):
            return nc.alloc_semaphore(f"{name}_c{layer}")

        acc = ctx.enter_context(nc.sbuf_tensor(f"acc_c{layer}", [P, NT, D], F32))
        g2 = ctx.enter_context(nc.sbuf_tensor(f"g2_c{layer}", [P, streams, D], F32))
        g2_in, gated, x_done, x_out = sem("g2_in"), sem("gated"), sem("x_done"), sem("x_out")
        acc_in = [sem(f"acc_in{t}") for t in range(NT)]
        block = ctx.enter_context(nc.Block())

        @block.sync
        def _(sp):
            for s in range(streams):
                sp.dma_start(g2[:, s, :], io['modrow'][layer, s:s + 1, 5 * D:6 * D].to_broadcast([P, D])).then_inc(g2_in, 16)
            for t in range(NT):
                sp.dma_start(acc[:, t, :], acc_dram[t * P:(t + 1) * P, :]).then_inc(acc_in[t], 16)
            for t in range(NT):
                sp.wait_ge(x_done, t + 1)
                for rows, dst in st['x_out'](t):
                    sp.dma_start(dst, x[rows, t, :]).then_inc(x_out, 16)
            sp.wait_ge(x_out, 16 * sum(len(st['x_out'](t)) for t in range(NT)))

        @block.vector
        def _(dve):
            dve.wait_ge(g2_in, 16 * streams)
            for t in range(NT):
                dve.wait_ge(acc_in[t], 16)
                dve.tensor_tensor(acc[:, t, :], acc[:, t, :], g2[:, 1 if t >= NT - ctx_tiles else 0, :], ALU.mult).then_inc(gated, 1)
                dve.wait_ge(gated, t + 1)
                dve.tensor_tensor(x[:, t, :], x[:, t, :], acc[:, t, :], ALU.add).then_inc(x_done, 1)



SG, SI, SP_, SL = 64, 16, 64, 8
NQ = SL + 1
GB = 8
TWO_PI = 2.0 * math.pi
PI_PARTS = (6.28125, float(np.float32(TWO_PI - 6.28125)),
            float(TWO_PI - 6.28125 - float(np.float32(TWO_PI - 6.28125))))
PI_SAFE = 3.1415925
ROUND = 1.5 * 2 ** 23


def prepare(nc, io):
    NC = 6 * D // 512
    ctx = ExitStack()
    with nc.cleanup_on_exit(), ctx:
        def sb(name, shape, dt=F32):
            return ctx.enter_context(nc.sbuf_tensor(f"{name}_p", shape, dt))

        def sem(name):
            return nc.alloc_semaphore(f"{name}_p")

        craw = sb("craw", [P, 2, KD])
        cT = sb("cT", [P, KD, 2])
        w = [sb(f"w{b}", [P, KD, 512]) for b in range(3)]
        row = [sb(f"row{b}", [2, 512]) for b in range(3)]
        fold = sb("fold", [P, 2, 4 * 6 * D // P])
        ident = sb("ident", [P, P])
        araw = sb("araw", [SG, 3, 2, SP_])
        ccraw = sb("ccraw", [P, 2, 8, 2, SP_])
        par = sb("par", [P, 3, SG])
        v = sb("v", [P, 16, SG])
        C = sb("C", [P, 2, SG, SI])
        B = sb("B", [P, 2, SG, SI])
        Bb = sb("Bb", [P, 2, SG, SI])
        tB = sb("tB", [P, SG, SI])
        Bd = [B, ccraw[:].rearrange("p a t d n -> p (a t d n)").rearrange("p (a g j) -> p a g j", a=2, g=SG)]
        N = sb("N", [P, 2, NQ, SG])
        Pw = sb("Pw", [P, 2, NQ, SG])
        L8 = sb("L8", [P, 2, 2, SG])
        Wt = [sb(f"Wt{b}", [P, 2, GB, NQ, SI]) for b in range(2)]
        Wm = sb("Wm", [P, 2, GB, NQ, SI])
        Rt = [sb(f"Rt{b}", [P, 2, GB, SL, SI]) for b in range(2)]
        Rm = [sb(f"Rm{b}", [P, 2, GB, SL, SI]) for b in range(2)]
        RT = [sb(f"RT{b}", [P, 4, 2, P]) for b in range(2)]
        KT = [sb(f"KT{b}", [SI, 4, 15 * SI]) for b in range(2)]
        acc = [ctx.enter_context(nc.psum_tensor(f"acc{b}_p", [2, 512], F32)) for b in range(3)]
        pR = ctx.enter_context(nc.psum_tensor("pR_p", [P, 1024], F32))
        pK = ctx.enter_context(nc.psum_tensor("pK_p", [P, 1024], F32))
        names = ("c_in c_done a_in cc_in b_in id0 id1 mm par_mm par_done c_mm c_copied step_done ang_done "
                 "sin_done exp_done bb_done bd_done pw_done l8_out w_done rm_done r_done rt_mm rt_done kt_mm kt_done "
                 "fold_in folded mod_out row_done chain")
        S = {n: sem(n) for n in names.split()}
        w_in = [sem(f"w_in{b}") for b in range(3)]
        row_out = [sem(f"row_out{b}") for b in range(3)]
        w_out = [sem(f"w_out{b}") for b in range(2)]
        rt_out = [sem(f"rt_out{b}") for b in range(2)]
        kt_out = [sem(f"kt_out{b}") for b in range(2)]
        block = ctx.enter_context(nc.Block())
        wm = io['mod_w'].rearrange("l (p k) n -> l p k n", k=KD)
        NCH, NB = 2 * NC, SG // GB
        HEAD = 8
        ORDER = [('chunk', n) for n in range(HEAD)]
        for b in range(NB):
            ORDER += [('batch', b)] + [('chunk', HEAD + 2 * b + j) for j in range(2)]
        assert len(ORDER) == NCH + NB

        def fold_view(dram):
            return dram.rearrange("l s n -> (l s n)").rearrange("(p c) -> p c", p=P)

        @block.sync
        def _(sp):
            sp.dma_start(craw[:, 0, :], io['c'].rearrange("o (p k) -> (o p) k", k=KD)).then_inc(S['c_in'], 16)
            sp.dma_start(craw[:, 1, :], io['c_ctx'].rearrange("(p k) -> p k", k=KD)).then_inc(S['c_in'], 16)
            for j, n in enumerate(('s5_a_re', 's5_a_im', 's5_log_step')):
                sp.dma_start(araw[:, j], io[n][0].rearrange("d g p -> g d p")).then_inc(S['a_in'], 16)
            for n in range(NCH):
                if n >= 3:
                    sp.wait_ge(S['mm'], n - 2)
                c = (n % NC) * 512
                sp.dma_start(w[n % 3][:], wm[n // NC, :, :, c:c + 512]).then_inc(w_in[n % 3], 16)

        @block.gpsimd
        def _(pool):
            pool.memset(ident[:], 0.0).then_inc(S['id0'], 1)
            for part, n in enumerate(('s5_c_re', 's5_c_im')):
                for d in range(2):
                    pool.dma_start(ccraw[:, part, :, d, :], io[n][0, d].rearrange("(t a) i p -> (a i) t p", a=8)).then_inc(S['cc_in'], 16)
            for part, n in enumerate(('s5_b_re', 's5_b_im')):
                for d in range(2):
                    pool.dma_start(B[d * 64:d * 64 + 64, part], io[n][0, d].rearrange("g p j -> p g j")).then_inc(S['b_in'], 16)
            pool.wait_ge(S['id0'], 1)
            pool.affine_select(out=ident[:], in_=ident[:], compare_op=ALU.not_equal, fill=1.0, base=0,
                               pattern=[[-1, P]], channel_multiplier=1).then_inc(S['id1'], 1)
            pool.wait_ge(S['bb_done'], 1)
            pool.wait_ge(S['pw_done'], 1)
            for b in range(NB):
                if b >= 2:
                    pool.wait_ge(S['r_done'], 2 * (b - 1))
                    pool.wait_ge(S['rt_mm'], 2 * (b - 1))
                g = slice(b * GB, (b + 1) * GB)
                for part in range(2):
                    for m, dst in enumerate((Rt, Rm)):
                        slots = Pw[:, m if part == 0 else 1 - m, SL:0:-1, g]
                        pool.tensor_tensor(dst[b % 2][:, part], slots.rearrange("p k (g o) -> p g k o", o=1).to_broadcast([P, GB, SL, SI]),
                                           Bb[:, m, g, :].rearrange("p g (o j) -> p g o j", o=1).to_broadcast([P, GB, SL, SI]),
                                           ALU.mult).then_inc(S['rm_done'], 1)

        @block.scalar
        def _(act):
            act.wait_ge(S['c_in'], 32)
            act.activation(cT[:], craw[:].rearrange("p s k -> p k s"), ACT.Silu).then_inc(S['c_done'], 1)
            act.wait_ge(S['par_done'], 1)
            act.activation(v[:, 0], par[:, 2], ACT.Exp).then_inc(S['step_done'], 1)
            for kind, n in ORDER:
                if (kind, n) == ('chunk', 2):
                    act.wait_ge(S['ang_done'], 1)
                    act.activation(v[:, 1], v[:, 1], ACT.Exp).then_inc(S['exp_done'], 1)
                    for j in (2, 3):
                        act.activation(v[:, j], v[:, j], ACT.Sin).then_inc(S['sin_done'], 1)
                    act.wait_ge(S['c_mm'], 2)
                    act.activation(C[:, 0], pR[:].rearrange("p (g i) -> p g i", i=SI), ACT.Copy).then_inc(S['c_copied'], 1)
                    act.activation(C[:, 1], pK[:].rearrange("p (g i) -> p g i", i=SI), ACT.Copy).then_inc(S['c_copied'], 1)
                if kind == 'chunk':
                    act.wait_ge(S['mm'], n + 1)
                    if n >= 3:
                        act.wait_ge(row_out[n % 3], 16 * (n // 3))
                    act.activation(row[n % 3][:], acc[n % 3][:], ACT.Copy).then_inc(S['row_done'], 1)
                    act.wait_ge(S['row_done'], n + 1)
                    c = (n % NC) * 512
                    act.dma_start(io['modraw'][n // NC, :, c:c + 512], row[n % 3][:]).then_inc(row_out[n % 3], 16)
                    continue
                g0 = n * GB
                act.wait_ge(S['w_done'], 2 * (n + 1))
                act.dma_start(io['s5_w'][:, n], Wt[n % 2][:].rearrange("p a g k i -> p (a g k i)")).then_inc(w_out[n % 2], 16)
                for half in range(2):
                    at = 2 * n + half
                    act.wait_ge(S['rt_mm'], at + 1)
                    if n:
                        act.wait_ge(rt_out[half], 16 * n)
                        act.wait_ge(kt_out[half], 16 * n)
                    act.activation(RT[half][:], pR[:].rearrange("p (g t c) -> p g t c", g=4, t=2), ACT.Copy).then_inc(S['rt_done'], 1)
                    act.wait_ge(S['kt_mm'], at + 1)
                    act.activation(KT[half][:], pK[0:SI, :].rearrange("p (g c) -> p g c", g=4)[:, :, 0:15 * SI],
                                   ACT.Copy).then_inc(S['kt_done'], 1)
                    act.wait_ge(S['rt_done'], at + 1)
                    act.dma_start(io['s5_r'][:, at], RT[half][:].rearrange("p g t c -> p (g t c)")).then_inc(rt_out[half], 16)
                    act.wait_ge(S['kt_done'], at + 1)
                    act.dma_start(io['s5_kt'][g0 + 4 * half:g0 + 4 * half + 4].rearrange("g j c -> j g c"), KT[half][:])\
                       .then_inc(kt_out[half], 16)
            for b in range(3):
                act.wait_ge(row_out[b], 16 * (NCH // 3))
            act.dma_start(fold[:, 0], fold_view(io['modraw'])).then_inc(S['fold_in'], 16)
            for layer in range(2):
                for s in range(2):
                    act.dma_start(fold[(2 * layer + s) * 32:(2 * layer + s) * 32 + 32, 1],
                                  io['mod_b'][layer].rearrange("(p c) -> p c", p=32)).then_inc(S['fold_in'], 16)
            act.wait_ge(S['folded'], 1)
            act.dma_start(fold_view(io['modrow']), fold[:, 0]).then_inc(S['mod_out'], 16)
            act.wait_ge(S['pw_done'], 2)
            act.dma_start(io['s5_l8'], L8[:].rearrange("p a b g -> p (a b g)")).then_inc(S['l8_out'], 16)
            act.wait_ge(S['mod_out'], 16)
            act.wait_ge(S['l8_out'], 16)
            for b in range(2):
                act.wait_ge(w_out[b], 16 * (NB // 2))
                act.wait_ge(rt_out[b], 16 * NB)
                act.wait_ge(kt_out[b], 16 * NB)

        @block.vector
        def _(dve):
            done = Counter(dve, S['chain'])
            t4 = v[:, 4]
            dve.wait_ge(S['par_mm'], 1)
            dve.tensor_copy(par[:], pR[:, 0:3 * SG].rearrange("p (j g) -> p j g", j=3)).then_inc(S['par_done'], 1)
            dve.wait_ge(S['par_done'], 1)
            re, im, step = par[:, 0], par[:, 1], v[:, 0]
            done(dve.tensor_scalar(re, re, -1e-4, None, ALU.min))
            done.wait()
            dve.wait_ge(S['step_done'], 1)
            done(dve.tensor_tensor(v[:, 1], re, step, ALU.mult))
            done(dve.tensor_tensor(t4, im, step, ALU.mult))
            done.wait()
            for j, turn in ((2, 0.0), (3, 0.25)):
                done(dve.tensor_scalar(v[:, j], t4, 1.0 / TWO_PI, turn, ALU.mult, ALU.add))
                done.wait()
                done(dve.tensor_scalar(v[:, 5], v[:, j], ROUND, None, ALU.add))
                done.wait()
                done(dve.tensor_scalar(v[:, 5], v[:, 5], -ROUND, None, ALU.add))
                done.wait()
                done(dve.scalar_tensor_tensor(out=v[:, j], in0=v[:, 5], scalar=-PI_PARTS[0], in1=t4, op0=ALU.mult, op1=ALU.add))
                done.wait()
                for part in PI_PARTS[1:]:
                    done(dve.scalar_tensor_tensor(out=v[:, j], in0=v[:, 5], scalar=-part, in1=v[:, j], op0=ALU.mult, op1=ALU.add))
                    done.wait()
                if turn:
                    done(dve.tensor_scalar(v[:, j], v[:, j], math.pi / 2, None, ALU.add))
                    done.wait()
                done(dve.tensor_scalar(v[:, j], v[:, j], PI_SAFE, -PI_SAFE, ALU.min, ALU.max))
                done.wait()
            dve.sem_inc(S['ang_done'], 1)
            dve.wait_ge(S['exp_done'], 1)
            dve.wait_ge(S['sin_done'], 2)
            one_re, one_im = N[:, 0, 1], N[:, 1, 1]
            done(dve.tensor_tensor(one_re, v[:, 1], v[:, 3], ALU.mult))
            done(dve.tensor_tensor(one_im, v[:, 1], v[:, 2], ALU.mult))
            done(dve.memset(N[:, 0, 0], 1.0))
            done(dve.memset(N[:, 1, 0], 0.0))
            done.wait()
            done(dve.tensor_scalar(v[:, 5], one_re, -1.0, None, ALU.add))
            done(dve.tensor_tensor(v[:, 6], re, re, ALU.mult))
            done(dve.tensor_tensor(v[:, 7], im, im, ALU.mult))
            done.wait()
            done(dve.tensor_tensor(v[:, 6], v[:, 6], v[:, 7], ALU.add))
            done(dve.tensor_tensor(v[:, 8], v[:, 5], re, ALU.mult))
            done(dve.tensor_tensor(v[:, 9], one_im, im, ALU.mult))
            done(dve.tensor_tensor(v[:, 10], one_im, re, ALU.mult))
            done(dve.tensor_tensor(v[:, 11], v[:, 5], im, ALU.mult))
            done.wait()
            done(dve.reciprocal(v[:, 6], v[:, 6]))
            done(dve.tensor_tensor(v[:, 8], v[:, 8], v[:, 9], ALU.add))
            done(dve.tensor_tensor(v[:, 10], v[:, 10], v[:, 11], ALU.subtract))
            done.wait()
            done(dve.tensor_tensor(v[:, 8], v[:, 8], v[:, 6], ALU.mult))
            done(dve.tensor_tensor(v[:, 9], v[:, 10], v[:, 6], ALU.mult))
            for k in range(2, NQ):
                done.wait()
                done(dve.tensor_tensor(v[:, 12], N[:, 0, k - 1], one_re, ALU.mult))
                done(dve.tensor_tensor(v[:, 13], N[:, 1, k - 1], one_im, ALU.mult))
                done(dve.tensor_tensor(v[:, 14], N[:, 0, k - 1], one_im, ALU.mult))
                done(dve.tensor_tensor(v[:, 15], N[:, 1, k - 1], one_re, ALU.mult))
                done.wait()
                done(dve.tensor_tensor(N[:, 0, k], v[:, 12], v[:, 13], ALU.subtract))
                done(dve.tensor_tensor(N[:, 1, k], v[:, 14], v[:, 15], ALU.add))
            dve.wait_ge(S['b_in'], 64)
            qre, qim = (v[:, j].rearrange("p (g o) -> p g o", o=1).to_broadcast([P, SG, SI]) for j in (8, 9))
            done.wait()
            done(dve.tensor_tensor(Bb[:, 0], B[:, 0], qre, ALU.mult))
            done(dve.tensor_tensor(tB[:], B[:, 1], qim, ALU.mult))
            done(dve.tensor_tensor(Bb[:, 1], B[:, 1], qre, ALU.mult))
            done.wait()
            done(dve.tensor_tensor(Bb[:, 0], Bb[:, 0], tB[:], ALU.subtract))
            done.wait()
            done(dve.tensor_tensor(tB[:], B[:, 0], qim, ALU.mult))
            done.wait()
            dve.tensor_tensor(Bb[:, 1], Bb[:, 1], tB[:], ALU.add).then_inc(S['bb_done'], 1)
            dve.wait_ge(S['bb_done'], 1)
            dve.wait_ge(S['c_mm'], 2)
            for d in range(2):
                mine, other = slice(64 * d, 64 * d + 64), slice(64 - 64 * d, P - 64 * d)
                dve.tensor_copy(Bd[d][mine], Bb[mine]).then_inc(S['bd_done'], 1)
                dve.memset(Bd[d][other], 0.0).then_inc(S['bd_done'], 1)
            done(dve.tensor_copy(Pw[0:64], N[0:64]))
            done(dve.tensor_copy(Pw[64:P], N[64:P, :, ::-1, :]))
            done.wait()
            dve.sem_inc(S['pw_done'], 1)
            for part in range(2):
                done(dve.tensor_copy(L8[:, 0, part], N[:, 0, SL]))
                done(dve.tensor_scalar(L8[:, 1, part], N[:, 1, SL], -1.0 if part else 1.0, None, ALU.mult))
            done.wait()
            dve.sem_inc(S['pw_done'], 1)
            dve.wait_ge(S['c_copied'], 2)
            for b in range(NB):
                h = b % 2
                if b >= 2:
                    dve.wait_ge(w_out[h], 16 * (b // 2))
                    dve.wait_ge(S['kt_mm'], 2 * (b - 1))
                g = slice(b * GB, (b + 1) * GB)

                def cb(part):
                    return C[:, part, g, :].rearrange("p g (o i) -> p g o i", o=1).to_broadcast([P, GB, NQ, SI])

                def pb(part):
                    return Pw[:, part, :, g].rearrange("p k (g o) -> p g k o", o=1).to_broadcast([P, GB, NQ, SI])

                done(dve.tensor_tensor(Wt[h][:, 0], pb(0), cb(0), ALU.mult))
                done(dve.tensor_tensor(Wm[:, 0], pb(1), cb(1), ALU.mult))
                done(dve.tensor_tensor(Wt[h][:, 1], pb(1), cb(0), ALU.mult))
                done(dve.tensor_tensor(Wm[:, 1], pb(0), cb(1), ALU.mult))
                done.wait()
                flat = [Wt[h][:, part].rearrange("p g k i -> p (g k i)") for part in range(2)]
                mflat = [Wm[:, part].rearrange("p g k i -> p (g k i)") for part in range(2)]
                dve.tensor_tensor(flat[0], flat[0], mflat[0], ALU.subtract).then_inc(S['w_done'], 1)
                dve.scalar_tensor_tensor(out=flat[1], in0=flat[1], scalar=-1.0, in1=mflat[1], op0=ALU.mult,
                                         op1=ALU.subtract).then_inc(S['w_done'], 1)
                dve.wait_ge(S['w_done'], 2 * (b + 1))
                dve.wait_ge(S['rm_done'], 4 * (b + 1))
                for part, op in ((0, ALU.subtract), (1, ALU.add)):
                    dve.tensor_tensor(Rt[h][:, part], Rt[h][:, part], Rm[h][:, part], op).then_inc(S['r_done'], 1)
            dve.wait_ge(S['fold_in'], 16 * 5)
            dve.tensor_tensor(fold[:, 0], fold[:, 0], fold[:, 1], ALU.add).then_inc(S['folded'], 1)

        @block.tensor
        def _(pe):
            pe.wait_ge(S['id1'], 1)
            pe.wait_ge(S['a_in'], 48)
            for j in range(3):
                last = pe.transpose(pR[:, j * SG:(j + 1) * SG], araw[:, j].rearrange("g d p -> g (d p)"), ident[0:SG, 0:SG])
            last.then_inc(S['par_mm'], 1)
            pe.wait_ge(S['c_done'], 1)
            for kind, n in ORDER:
                if (kind, n) == ('chunk', 2):
                    pe.wait_ge(S['cc_in'], 64)
                    pe.wait_ge(S['par_done'], 1)
                    for part, dst in enumerate((pR, pK)):
                        for t in range(8):
                            last = pe.transpose(dst[:, t * P:(t + 1) * P], ccraw[:, part, t].rearrange("a d p -> a (d p)"), ident[:])
                        last.then_inc(S['c_mm'], 1)
                if kind == 'chunk':
                    pe.wait_ge(w_in[n % 3], 16 * (n // 3 + 1))
                    if n >= 3:
                        pe.wait_ge(S['row_done'], n - 2)
                    for k in range(KD):
                        last = pe.matmul(acc[n % 3][:], cT[:, k, :], w[n % 3][:, k, :], start=(k == 0), stop=(k == KD - 1))
                    last.then_inc(S['mm'], 1)
                    continue
                h = n % 2
                for half in range(2):
                    at = 2 * n + half
                    if at == 0:
                        pe.wait_ge(S['c_copied'], 2)
                        pe.wait_ge(S['bd_done'], 4)
                    else:
                        pe.wait_ge(S['rt_done'], at)
                    pe.wait_ge(S['r_done'], 2 * (n + 1))
                    for g in range(4):
                        for part in range(2):
                            last = pe.transpose(pR[:, (2 * g + part) * P:(2 * g + part + 1) * P],
                                                Rt[h][:, part, 4 * half + g].rearrange("p s j -> p (s j)"), ident[:])
                    last.then_inc(S['rt_mm'], 1)
                    if at:
                        pe.wait_ge(S['kt_done'], at)
                    pe.wait_ge(S['w_done'], 2 * (n + 1))
                    for g in range(4):
                        gg = n * GB + 4 * half + g
                        for d, k0, c0 in ((1, 1, 0), (0, 0, 7 * SI)):
                            for part in range(2):
                                last = pe.matmul(pK[0:SI, g * 256 + c0:g * 256 + c0 + SL * SI], Bd[d][:, part, gg, :],
                                                 Wt[h][:, part, 4 * half + g, k0:k0 + SL, :].rearrange("p k i -> p (k i)"),
                                                 start=(d == 1 and part == 0), stop=(d == 0 and part == 1),
                                                 skip_group_check=True)
                    last.then_inc(S['kt_mm'], 1)


def s5_mixer(nc, io, st):
    NCL, NCC = 64, 32
    NCK = NCL + NCC
    x = st['x']
    xin = io['x_mid']
    ctx = ExitStack()
    with nc.cleanup_on_exit(), ctx:
        def sb(name, shape, dt=F32):
            return ctx.enter_context(nc.sbuf_tensor(f"{name}_s", shape, dt))

        def sem(name):
            return nc.alloc_semaphore(f"{name}_s")

        XS = sb("XS", [P, SL * D])
        X = XS[0:NCK].rearrange("p (t d) -> p t d", t=SL)
        SV = XS[:].rearrange("p (a g c) -> p a g c", a=2, g=SG)
        Zc = X[0:NCL]
        UV = sb("UV", [P, (NCK * SG) + NCK * 2 * SG])
        U = UV[:, 0:NCK * SG].rearrange("p (g c) -> p g c", c=NCK)
        VH = UV[:, NCK * SG:].rearrange("p (n a g) -> p n a g", a=2, g=SG)
        glu = UV[:, 0:KD * 2 * D].rearrange("p (k n) -> p k n", k=KD)
        ZU = sb("ZU", [P, 2, SG * NCL])
        Xn = ZU[0:NCK].rearrange("p a n -> p (a n)").rearrange("p (g t j) -> p g t j", t=SL, j=SI)
        Z, UD = (ZU[:, j].rearrange("p (g c) -> p g c", c=NCL) for j in range(2))
        zT = ZU[:, 1].rearrange("p (k n) -> p k n", k=KD)
        Rb = [sb(f"Rb{b}", [P, 4, 2, P]) for b in range(3)]
        Wb = [sb(f"Wb{b}", [P, 2, GB, NQ, SI]) for b in range(2)]
        Tb = [sb(f"Tb{b}", [P, GB, P]) for b in range(2)]
        vec = sb("vec", [SG, 6, SI])
        vrep = sb("vrep", [SG, 6, SL, SI])
        vcol = sb("vcol", [P, 6, SG])
        l8 = sb("l8", [P, 2, 2, SG])
        ss = sb("ss", [NCK, SL])
        t1 = [sb(f"t1{b}", [P, 2, SG]) for b in range(2)]
        t2 = [sb(f"t2{b}", [P, 2, SG]) for b in range(2)]
        ident = sb("ident", [P, P])
        gb = x[:, NL:NL + 2, :].rearrange("p t d -> p (t d)")
        g1 = UV[:, KD * 2 * D:KD * 2 * D + D]
        sv, sg = ([Rb[j][:].rearrange("p g t c -> p (g t c)")[:, b * 512:(b + 1) * 512] for b in range(2)] for j in range(2))
        ps = ctx.enter_context(nc.psum_tensor("ps_s", [P, 8 * 512], F32))
        names = ("x_in xres_in vec_in l8_in gb_in id0 id1 sq_done var_done sd_done xn_done rep_done vec_mm vec_done "
                 "uT_mm u_mul u_done v_mm va_done vd_done rec t_mm sf_done sb_done o_mm ud_done zs_done z_done zT1_mm zc_act zc_dve "
                 "zT2_mm zt_act zt_dve glu_mm sg_pre sg_done out_used chain glu_in0 glu_in1")
        S = {n: sem(n) for n in names.split()}
        r_in = [sem(f"r_in{b}") for b in range(3)]
        w_in = [sem(f"w_in{b}") for b in range(2)]
        t_in = [sem(f"t_in{b}") for b in range(2)]
        block = ctx.enter_context(nc.Block())
        NHB, NB = SG // 4, SG // GB

        def zc_in(j):
            return ps[0:NCL, (j % 2) * 2048:(j % 2 + 1) * 2048].rearrange("p (g t i) -> p g t i", t=SL, i=SI)

        def zc_out(j):
            return Zc[:, :, j * 256:(j + 1) * 256].rearrange("p t (g i) -> p g t i", i=SI)

        @block.sync
        def _(sp):
            sp.dma_start(X[:], xin.rearrange("(c t) d -> c t d", t=SL)).then_inc(S['x_in'], 16)
            for s in range(2):
                sp.dma_start(vec[:, 2 * s:2 * s + 2], io['modrow'][1, s, 0:2 * D].rearrange("(a g j) -> g a j", a=2, j=SI)).then_inc(S['vec_in'], 16)
            sp.dma_start(vec[:, 4], io['norm1_g'][1].rearrange("(g j) -> g j", j=SI)).then_inc(S['vec_in'], 16)
            sp.dma_start(vec[:, 5], io['s5_d'][0].rearrange("(g j) -> g j", j=SI)).then_inc(S['vec_in'], 16)
            sp.dma_start(l8[:].rearrange("p a b g -> p (a b g)"), io['s5_l8']).then_inc(S['l8_in'], 16)
            for hb in range(NHB):
                if hb >= 3:
                    sp.wait_ge(S['v_mm'], hb - 2)
                sp.dma_start(Rb[hb % 3][:].rearrange("p g t c -> p (g t c)"), io['s5_r'][:, hb]).then_inc(r_in[hb % 3], 16)
            for b in range(2):
                sp.dma_start(Wb[b][:].rearrange("p a g k i -> p (a g k i)"), io['s5_w'][:, b]).then_inc(w_in[b], 16)
            for m in range(NL):
                for hh in range(2):
                    sp.dma_start(x[hh * 64:hh * 64 + 64, m, :],
                                 xin[0:LAT].rearrange("(c t) d -> t c d", t=SL)[2 * m + hh]).then_inc(S['xres_in'], 16)
            sp.dma_start(gb, io['s5_glu_b'].to_broadcast([P, 2 * D])).then_inc(S['gb_in'], 16)
            for b in range(2, NB):
                sp.wait_ge(S['o_mm'], b - 1)
                sp.dma_start(Wb[b % 2][:].rearrange("p a g k i -> p (a g k i)"), io['s5_w'][:, b]).then_inc(w_in[b % 2], 16)
            sp.wait_ge(S['o_mm'], NB)
            sp.wait_ge(S['ud_done'], 1)
            sp.dma_start(g1, io['modrow'][1, 0:1, 2 * D:3 * D].to_broadcast([P, D])).then_inc(S['gb_in'], 16)
            gw = io['s5_glu_w'][0].rearrange("(p k) n -> p k n", k=KD)
            for n in range(2):
                for half in range(2):
                    c = half * D + n * 512
                    sp.dma_start(glu[:, :, c:c + 512], gw[:, :, c:c + 512]).then_inc(S[f'glu_in{n}'], 16)

        @block.gpsimd
        def _(pool):
            pool.memset(ident[:], 0.0).then_inc(S['id0'], 1)
            pool.wait_ge(S['id0'], 1)
            pool.affine_select(out=ident[:], in_=ident[:], compare_op=ALU.not_equal, fill=1.0, base=0,
                               pattern=[[-1, P]], channel_multiplier=1).then_inc(S['id1'], 1)
            for b in range(NB):
                if b >= 2:
                    pool.wait_ge(S['t_mm'], b - 1)
                for s in range(SL):
                    pool.dma_start(Tb[b % 2][s * SI:(s + 1) * SI],
                                   io['s5_kt'][b * GB:(b + 1) * GB, :, (7 - s) * SI:(7 - s) * SI + P]
                                   .rearrange("g j c -> j g c")).then_inc(t_in[b % 2], 16)
            pool.wait_ge(S['u_done'], 16)
            pool.wait_ge(S['vec_done'], 1)
            pool.tensor_tensor(UD, U[:, :, 0:NCL], vcol[:, 5].rearrange("p (g o) -> p g o", o=1).to_broadcast([P, SG, NCL]),
                               ALU.mult).then_inc(S['ud_done'], 1)

        @block.scalar
        def _(act):
            act.wait_ge(S['x_in'], 16)
            for s in range(SL):
                if s:
                    act.wait_ge(S['sq_done'], s)
                act.activation(UV[0:NCK, 0:D], X[:, s, :], ACT.Square,
                               accum_out=ss[:, s:s + 1]).then_inc(S['sq_done'], 1)
            act.wait_ge(S['var_done'], 1)
            act.activation(ss[:], ss[:], ACT.Sqrt).then_inc(S['sd_done'], 1)
            for hb in range(NHB):
                act.wait_ge(S['v_mm'], hb + 1)
                src = ps[0:64, (hb % 4) * 1024:(hb % 4 + 1) * 1024].rearrange("p (g e) -> p g e", g=4)[:, :, 0:2 * NCK]\
                    .rearrange("p g (a c) -> p g a c", a=2)
                gs = slice(4 * hb, 4 * hb + 4)
                act.activation(VH[0:64, NCC:NCK, :, gs].rearrange("p c a g -> p g a c"), src[:, :, :, 0:NCL], ACT.Copy).then_inc(S['va_done'], 1)
                act.activation(VH[0:64, 0:NCC, :, gs].rearrange("p c a g -> p g a c"), src[:, :, :, NCL:NCK], ACT.Copy).then_inc(S['va_done'], 1)
            act.wait_ge(S['rec'], 4 * 94 + 1)
            for b in range(NB):
                g = slice(b * GB, (b + 1) * GB)
                act.activation(SV[0:64, :, g, :], VH[0:64, NCC - 1:NCK - 1, :, g].rearrange("p c a g -> p a g c"),
                               ACT.Copy).then_inc(S['sf_done'], 1)
            for b in range(NB):
                act.wait_ge(S['zs_done'], b + 1)
                act.activation(Z[:, b * GB:(b + 1) * GB, :], Z[:, b * GB:(b + 1) * GB, :], ACT.Gelu_apprx_tanh).then_inc(S['z_done'], 1)
            for j in (1, 3):
                act.wait_ge(S['zT1_mm'], j + 1)
                act.activation(zc_out(j), zc_in(j), ACT.Copy).then_inc(S['zc_act'], 1)
            for k in range(1, KD, 2):
                act.wait_ge(S['zT2_mm'], k + 1)
                act.activation(zT[:, k, :], ps[:, k * 512:(k + 1) * 512], ACT.Copy).then_inc(S['zt_act'], 1)
            for u in range(8):
                act.wait_ge(S['sg_pre'], u + 1)
                act.activation(sg[u % 2], sg[u % 2], ACT.Sigmoid).then_inc(S['sg_done'], 1)

        @block.vector
        def _(dve):
            done = Counter(dve, S['chain'])
            dve.wait_ge(S['vec_in'], 64)
            for s in range(2):
                done(dve.scalar_tensor_tensor(out=vec[:, 2 * s + 1], in0=vec[:, 2 * s + 1], scalar=1.0, in1=vec[:, 4],
                                              op0=ALU.add, op1=ALU.mult))
            done.wait()
            for j in range(6):
                done(dve.tensor_copy(vrep[:, j], vec[:, j:j + 1, :].to_broadcast([SG, SL, SI])))
            done.wait()
            dve.sem_inc(S['rep_done'], 1)
            dve.wait_ge(S['sq_done'], SL)
            done(dve.tensor_scalar(ss[:], ss[:], 1.0 / D, EPS, ALU.mult, ALU.add))
            done.wait()
            dve.reciprocal(ss[:], ss[:]).then_inc(S['var_done'], 1)
            dve.wait_ge(S['sd_done'], 1)
            for s in range(SL):
                dve.tensor_scalar(Xn[:, :, s, :], X[:, s, :].rearrange("p (g j) -> p g j", j=SI), ss[:, s:s + 1], None,
                                  ALU.mult).then_inc(S['xn_done'], 1)
            dve.wait_ge(S['vec_mm'], 1)
            dve.tensor_copy(vcol[:], ps[:, 7 * 512:7 * 512 + 6 * SG].rearrange("p (j g) -> p j g", g=SG)).then_inc(S['vec_done'], 1)
            dve.wait_ge(S['vec_done'], 1)
            for j in range(4):
                dve.wait_ge(S['uT_mm'], j + 1)
                src = ps[:, (j % 2) * 2048:(j % 2 + 1) * 2048].rearrange("p (b e) -> p b e", b=4)[:, :, 0:4 * NCK]\
                    .rearrange("p b (g c) -> p b g c", g=4)
                dst = U[:, j * 16:(j + 1) * 16, :].rearrange("p (b g) c -> p b g c", b=4)

                def vb(which, n):
                    return vcol[:, which, j * 16:(j + 1) * 16].rearrange("p (b g o) -> p b g o", b=4, o=1).to_broadcast([P, 4, 4, n])

                for s, c in ((0, slice(0, NCL)), (1, slice(NCL, NCK))):
                    dve.tensor_tensor(dst[:, :, :, c], src[:, :, :, c], vb(2 * s + 1, c.stop - c.start), ALU.mult).then_inc(S['u_mul'], 1)
                dve.wait_ge(S['u_mul'], 2 * (j + 1))
                for s, c in ((0, slice(0, NCL)), (1, slice(NCL, NCK))):
                    dve.tensor_tensor(dst[:, :, :, c], dst[:, :, :, c], vb(2 * s, c.stop - c.start), ALU.add).then_inc(S['u_done'], 2)
            for hb in range(NHB):
                dve.wait_ge(S['v_mm'], hb + 1)
                src = ps[64:P, (hb % 4) * 1024:(hb % 4 + 1) * 1024].rearrange("p (g e) -> p g e", g=4)[:, :, 0:2 * NCK]\
                    .rearrange("p g (a c) -> p g a c", a=2)
                gs = slice(4 * hb, 4 * hb + 4)
                dve.tensor_copy(VH[64:P, NCK - 1:NCC - 1:-1, :, gs].rearrange("p c a g -> p g a c"), src[:, :, :, 0:NCL]).then_inc(S['vd_done'], 1)
                dve.tensor_copy(VH[64:P, NCC - 1::-1, :, gs].rearrange("p c a g -> p g a c")[:, :, :, 0:NCC], src[:, :, :, NCL:NCK]).then_inc(S['vd_done'], 1)
            dve.wait_ge(S['l8_in'], 16)
            dve.wait_ge(S['va_done'], 2 * NHB)
            dve.wait_ge(S['vd_done'], 2 * NHB)
            dve.sem_inc(S['rec'], 1)
            with dve.Fori(0, 47) as q:
                for b in range(2):
                    prev = VH[:, bass.ds(q * 2 + b, 1)].rearrange("p n a g -> p (n a) g")
                    here = VH[:, bass.ds(q * 2 + b + 1, 1)].rearrange("p n a g -> p (n a) g")
                    dve.wait_ge(S['rec'], q * 8 + 4 * b + 1)
                    dve.tensor_tensor(t1[b][:], prev, l8[:, 0], ALU.mult).then_inc(S['rec'], 1)
                    dve.tensor_tensor(t2[b][:], prev, l8[:, 1], ALU.mult).then_inc(S['rec'], 1)
                    dve.wait_ge(S['rec'], q * 8 + 4 * b + 2)
                    dve.tensor_tensor(t1[b][:], t1[b][:], here, ALU.add).then_inc(S['rec'], 1)
                    dve.wait_ge(S['rec'], q * 8 + 4 * b + 4)
                    dve.tensor_tensor(here, t1[b][:], t2[b][:, ::-1, :], ALU.add).then_inc(S['rec'], 1)
            dve.wait_ge(S['rec'], 4 * 94 + 1)
            for b in range(NB):
                g = slice(b * GB, (b + 1) * GB)
                dve.tensor_copy(SV[64:P, :, g, :], VH[64:P, NCK - 2:NCC - 2:-1, :, g].rearrange("p c a g -> p a g c"))\
                   .then_inc(S['sb_done'], 1)
            dve.wait_ge(S['ud_done'], 1)
            for b in range(NB):
                dve.wait_ge(S['o_mm'], b + 1)
                dve.tensor_tensor(Z[:, b * GB:(b + 1) * GB, :], ps[:, b * 512:(b + 1) * 512].rearrange("p (g c) -> p g c", g=GB),
                                  UD[:, b * GB:(b + 1) * GB, :], ALU.add).then_inc(S['zs_done'], 1)
            for j in (0, 2):
                dve.wait_ge(S['zT1_mm'], j + 1)
                dve.tensor_copy(zc_out(j), zc_in(j)).then_inc(S['zc_dve'], 1)
            for k in range(0, KD, 2):
                dve.wait_ge(S['zT2_mm'], k + 1)
                dve.tensor_copy(zT[:, k, :], ps[:, k * 512:(k + 1) * 512]).then_inc(S['zt_dve'], 1)
            dve.wait_ge(S['gb_in'], 32)
            dve.wait_ge(S['xres_in'], 16 * 8)
            for u in range(8):
                n, m = divmod(u, 4)
                val, gat = (ps[:, (2 * (u % 4) + j) * 512:(2 * (u % 4) + j + 1) * 512] for j in range(2))
                c = slice(n * 512, (n + 1) * 512)
                a, b = sv[u % 2], sg[u % 2]
                dve.wait_ge(S['glu_mm'], u + 1)
                dve.tensor_tensor(b, gat, gb[:, D + n * 512:D + (n + 1) * 512], ALU.add).then_inc(S['sg_pre'], 1)
                done(dve.tensor_tensor(a, val, gb[:, c], ALU.add))
                done.wait()
                dve.sem_inc(S['out_used'], 1)
                dve.wait_ge(S['sg_done'], u + 1)
                done(dve.tensor_tensor(a, a, b, ALU.mult))
                done.wait()
                done(dve.tensor_tensor(a, a, g1[:, c], ALU.mult))
                done.wait()
                done(dve.tensor_tensor(x[:, m, c], x[:, m, c], a, ALU.add))
            done.wait()

        @block.tensor
        def _(pe):
            pe.wait_ge(S['id1'], 1)
            pe.wait_ge(S['rep_done'], 1)
            for j in range(6):
                last = pe.transpose(ps[:, 7 * 512 + j * SG:7 * 512 + (j + 1) * SG], vrep[:, j].rearrange("g s j -> g (s j)"),
                                    ident[0:SG, 0:SG])
            last.then_inc(S['vec_mm'], 1)
            pe.wait_ge(S['xn_done'], SL)
            for j in range(4):
                if j == 1:
                    pe.wait_ge(S['vec_done'], 1)
                if j >= 2:
                    pe.wait_ge(S['u_mul'], 2 * (j - 1))
                for g in range(16):
                    at = (j % 2) * 2048 + (g // 4) * 512 + (g % 4) * NCK
                    gg = j * 16 + g
                    last = pe.transpose(ps[:, at:at + NCK], Xn[:, gg].rearrange("p t j -> p (t j)"), ident[0:NCK, 0:NCK])
                last.then_inc(S['uT_mm'], 1)
            for hb in range(NHB):
                pe.wait_ge(S['u_done'], 16)
                pe.wait_ge(r_in[hb % 3], 16 * (hb // 3 + 1))
                if hb >= 4:
                    pe.wait_ge(S['va_done'], 2 * (hb - 3))
                    pe.wait_ge(S['vd_done'], 2 * (hb - 3))
                for g in range(4):
                    for part in range(2):
                        at = (hb % 4) * 1024 + g * 256 + part * NCK
                        last = pe.matmul(ps[:, at:at + NCK], Rb[hb % 3][:, g, part, :], U[:, hb * 4 + g, :], start=True, stop=True)
                last.then_inc(S['v_mm'], 1)
            pe.wait_ge(S['va_done'], 2 * NHB)
            pe.wait_ge(S['vd_done'], 2 * NHB)
            for b in range(NB):
                pe.wait_ge(t_in[b % 2], 16 * SL * (b // 2 + 1))
                for g in range(GB):
                    gg = b * GB + g
                    last = pe.matmul(ps[:, gg * NCL:(gg + 1) * NCL], Tb[b % 2][:, g, :], U[:, gg, 0:NCL],
                                     start=(g == 0), stop=False, skip_group_check=True)
                last.then_inc(S['t_mm'], 1)
            for b in range(NB):
                pe.wait_ge(w_in[b % 2], 16 * (b // 2 + 1))
                pe.wait_ge(S['sf_done'], b + 1)
                pe.wait_ge(S['sb_done'], b + 1)
                for g in range(GB):
                    gg = b * GB + g
                    for part in range(2):
                        last = pe.matmul(ps[:, gg * NCL:(gg + 1) * NCL],
                                         Wb[b % 2][:, part, g, 0:SL, :].rearrange("p k i -> p (k i)"),
                                         SV[:, part, gg, :], start=False, stop=(part == 1), skip_group_check=True)
                last.then_inc(S['o_mm'], 1)
            pe.wait_ge(S['z_done'], NB)
            for j in range(4):
                if j >= 2:
                    pe.wait_ge(S['zc_dve' if j % 2 == 0 else 'zc_act'], 1)
                for g in range(16):
                    at = (j % 2) * 2048 + g * P
                    last = pe.transpose(ps[0:NCL, at:at + P], Z[:, j * 16 + g, :], ident[:])
                last.then_inc(S['zT1_mm'], 1)
            pe.wait_ge(S['zc_dve'], 2)
            pe.wait_ge(S['zc_act'], 2)
            for k in range(KD):
                for t in range(SL):
                    last = pe.transpose(ps[:, k * 512 + t * NCL:k * 512 + (t + 1) * NCL],
                                        Zc[:, t, :].rearrange("p (c k) -> p k c", k=KD)[:, k, :], ident[0:NCL, 0:NCL])
                last.then_inc(S['zT2_mm'], 1)
            pe.wait_ge(S['zt_act'], KD // 2)
            pe.wait_ge(S['zt_dve'], KD // 2)
            for u in range(8):
                n, m = divmod(u, 4)
                if m == 0:
                    pe.wait_ge(S[f'glu_in{n}'], 32)
                if u >= 4:
                    pe.wait_ge(S['out_used'], u - 3)
                    pe.wait_ge(S['sg_pre'], u - 3)
                for half in range(2):
                    for k in range(KD):
                        c = half * D + n * 512
                        last = pe.matmul(ps[:, (2 * (u % 4) + half) * 512:(2 * (u % 4) + half + 1) * 512],
                                         zT[:, k, m * P:(m + 1) * P], glu[:, k, c:c + 512], start=(k == 0), stop=(k == KD - 1))
                last.then_inc(S['glu_mm'], 1)



def program(nc, io, out):
    def dram(name, shape, dt=F32):
        return nc.dram_tensor(name, shape, dt).ap()

    with ExitStack() as ctx:
        x = ctx.enter_context(nc.sbuf_tensor("x", [P, NT0, D], F32))
        for name in ('modraw', 'modrow'):
            io[name] = dram(name, (2, 2, 6 * D))
        io['s5_r'] = dram('s5_r', (P, SG // 4, 4 * 2 * P))
        io['s5_w'] = dram('s5_w', (P, SG // GB, 2 * GB * NQ * SI))
        io['s5_kt'] = dram('s5_kt', (SG, SI, 15 * SI))
        io['s5_l8'] = dram('s5_l8', (P, 4 * SG))
        io['x_mid'] = dram('x_mid', (NTOK, D))
        moe_h, moe_acc, table = dram('moe_h', (NTOK, D)), dram('moe_acc', (NTOK, D)), dram('item_table', (P, 4), I32)

        def x_mid(t):
            return [(slice(0, P), io['x_mid'][t * P:(t + 1) * P, :])]

        def x_final(t):
            steps = out[0].rearrange("(c s) d -> s c d", s=SL)
            return [(slice(64 * j, 64 * j + 64), steps[2 * t + j]) for j in range(2)]

        prepare(nc, io)
        mixer0(nc, io, {'x': x})
        moe_blocks(nc, io, {'x': x, 'moe_h': moe_h, 'moe_acc': moe_acc, 'item_table': table, 'x_out': x_mid},
                   0, NTOK, NT0 - NL)
        s5_mixer(nc, io, {'x': x})
        moe_blocks(nc, io, {'x': x, 'moe_h': moe_h[0:LAT], 'moe_acc': moe_acc[0:LAT], 'item_table': table,
                            'x_out': x_final}, 1, LAT, 0)


def kernel(**inputs):
    import concourse.bacc as bacc
    from concourse.bass_utils import run_bass_kernel_spmd as run
    nc = bacc.Bacc("TRN2", target_bir_lowering=False, num_devices=1)
    inputs['rope'] = rope_tables()
    arrays, io = {}, {}
    for name, a in inputs.items():
        arrays[f"in_{name}"] = np.ascontiguousarray(a)
        io[name] = nc.dram_tensor(f"in_{name}", a.shape, F32, kind="ExternalInput").ap()
    out = nc.dram_tensor("out", (1, LAT, D), F32, kind="ExternalOutput").ap()
    program(nc, io, out)
    results = run(nc, [arrays], core_ids=[0])
    return results.results[0]["out"]
```
